# Optimizing a Trainium2 kernel written in Bass

```python
import math
import jax, jax.numpy as jnp
from jax import lax
import numpy as np

D_MODEL = 1024
BATCH = 1
SEQ = 256
DEPTH = 2

HEAD_DIM = 64
NSA_HEADS = 4
DIFF_HEADS = 4
FOX_HEADS = 8
NSA_WIDTH = NSA_HEADS * HEAD_DIM
DIFF_WIDTH = DIFF_HEADS * HEAD_DIM
FOX_WIDTH = FOX_HEADS * HEAD_DIM
MIX_WIDTH = NSA_WIDTH + DIFF_WIDTH + FOX_WIDTH
NSA_KV_HEADS = 1
NSA_GROUP = NSA_HEADS // NSA_KV_HEADS
NSA_BRANCHES = 3
CMP_BLOCK = 32
CMP_STRIDE = 16
CMP_HIDDEN = 256
SLC_BLOCK = 64
SLC_TOPK = 16
WINDOW = 512
DIFF_QK_DIM = HEAD_DIM // 2
DIFF_V_DIM = HEAD_DIM
D_FF = 2752
PLE_DIM = 256
ROPE_THETA = 10000.0
QUERY_BLOCK = 128
SLC_QUERY_BLOCK = 32
LN_EPS = 1e-5
NEG_BIG = -1e30
DEEPNORM_ALPHA = (2.0 * DEPTH) ** 0.25
DEEPNORM_BETA = (8.0 * DEPTH) ** -0.25
IN_SPLITS = (
    NSA_WIDTH,
    6 * NSA_KV_HEADS * HEAD_DIM,
    NSA_BRANCHES * NSA_HEADS,
    2 * DIFF_HEADS * DIFF_QK_DIM,
    2 * DIFF_HEADS * DIFF_QK_DIM,
    DIFF_HEADS * DIFF_V_DIM,
    FOX_WIDTH, FOX_WIDTH, FOX_WIDTH,
    FOX_HEADS,
)
IN_COLS = sum(IN_SPLITS)


def layer_norm(x, g, b):
    xf = x.astype(jnp.float32)
    mu = jnp.mean(xf, axis=-1, keepdims=True)
    var = jnp.mean(jnp.square(xf - mu), axis=-1, keepdims=True)
    return ((xf - mu) * lax.rsqrt(var + LN_EPS) * g.astype(jnp.float32) + b.astype(jnp.float32)).astype(x.dtype)

def rope(x, pos):
    d = x.shape[-1]
    inv = ROPE_THETA ** (-jnp.arange(0, d, 2, dtype=jnp.float32) / d)
    ang = pos.astype(jnp.float32)[:, None] * inv[None, :]
    cos = jnp.cos(ang)[:, None, :]
    sin = jnp.sin(ang)[:, None, :]
    xf = x.astype(jnp.float32)
    x1, x2 = xf[..., : d // 2], xf[..., d // 2:]
    return jnp.concatenate([x1 * cos - x2 * sin, x2 * cos + x1 * sin], axis=-1).astype(x.dtype)

def swiglu(x, w_gate, w_up, w_down):
    return (jax.nn.silu(x @ w_gate) * (x @ w_up)) @ w_down

def masked_softmax(s, mask):
    p = jax.nn.softmax(jnp.where(mask, s.astype(jnp.float32), NEG_BIG), axis=-1)
    return jnp.where(mask, p, 0.0)

def sweep(fn, n_blocks):
    out = jnp.moveaxis(lax.map(fn, jnp.arange(n_blocks)), 0, 1)
    return out.reshape((out.shape[0], -1) + out.shape[3:])

def cmp_to_slc_matrix(n_cmp, n_slc):
    c0 = np.arange(n_cmp) * CMP_STRIDE
    s0 = np.arange(n_slc) * SLC_BLOCK
    m = (c0[:, None] < s0[None, :] + SLC_BLOCK) & (c0[:, None] + CMP_BLOCK > s0[None, :])
    return jnp.asarray(m.astype(np.float32))

def nsa_attention(q, k_cmp, v_cmp, k_slc, v_slc, k_win, v_win, gates, pos_k, pos_v, phi_k1, phi_k2, phi_v1, phi_v2):
    B, S = q.shape[0], q.shape[1]
    scale = HEAD_DIM ** -0.5
    t = jnp.arange(S)
    n_cmp = (S - CMP_BLOCK) // CMP_STRIDE + 1
    starts = jnp.arange(n_cmp) * CMP_STRIDE
    idx = starts[:, None] + jnp.arange(CMP_BLOCK)[None, :]

    def compress(kv, pe, w1, w2):
        blk = kv[:, idx] + pe[:, None, :]
        blk = jnp.transpose(blk, (0, 1, 3, 2, 4)).reshape(B, n_cmp, NSA_KV_HEADS, CMP_BLOCK * HEAD_DIM)
        return jax.nn.gelu(blk @ w1) @ w2

    block_end = starts + CMP_BLOCK - 1
    kc = rope(compress(k_cmp, pos_k, phi_k1, phi_k2), block_end)
    vc = compress(v_cmp, pos_v, phi_v1, phi_v2)
    mask_c = block_end[None, :] <= t[:, None]
    s_c = jnp.einsum('bthgd,bchd->bhgtc', q, kc) * scale
    p_c = masked_softmax(s_c, mask_c)
    o_cmp = jnp.einsum('bhgtc,bchd->bthgd', p_c.astype(vc.dtype), vc)
    n_slc = S // SLC_BLOCK
    top = min(SLC_TOPK, n_slc)
    imp = jnp.sum(p_c, axis=2) @ cmp_to_slc_matrix(n_cmp, n_slc)
    j = jnp.arange(n_slc)[None, :]
    blk_t = (t // SLC_BLOCK)[:, None]
    forced = (j == 0) | (j == blk_t) | (j == blk_t - 1)
    valid = j * SLC_BLOCK <= t[:, None]
    score = jnp.where(forced, 1e9, jnp.where(valid, imp, -1.0))
    _, sel = lax.top_k(score, top)
    sel = jnp.transpose(sel, (0, 2, 1, 3))
    k_blk = jnp.transpose(k_slc.reshape(B, n_slc, SLC_BLOCK, NSA_KV_HEADS, HEAD_DIM), (0, 3, 1, 2, 4))
    v_blk = jnp.transpose(v_slc.reshape(B, n_slc, SLC_BLOCK, NSA_KV_HEADS, HEAD_DIM), (0, 3, 1, 2, 4))
    b_idx = jnp.arange(B)[:, None, None, None]
    h_idx = jnp.arange(NSA_KV_HEADS)[None, None, :, None]

    def slc_block(i):
        t0 = i * SLC_QUERY_BLOCK
        qb = lax.dynamic_slice_in_dim(q, t0, SLC_QUERY_BLOCK, axis=1)
        sb = lax.dynamic_slice_in_dim(sel, t0, SLC_QUERY_BLOCK, axis=1)
        kg = k_blk[b_idx, h_idx, sb]
        vg = v_blk[b_idx, h_idx, sb].reshape(B, SLC_QUERY_BLOCK, NSA_KV_HEADS, top * SLC_BLOCK, HEAD_DIM)
        key_pos = sb[..., None] * SLC_BLOCK + jnp.arange(SLC_BLOCK)
        tq = t0 + jnp.arange(SLC_QUERY_BLOCK)
        mask = (key_pos <= tq[None, :, None, None, None]).reshape(B, SLC_QUERY_BLOCK, NSA_KV_HEADS, 1, top * SLC_BLOCK)
        s = jnp.einsum('bqhgd,bqhkld->bqhgkl', qb, kg) * scale
        p = masked_softmax(s.reshape(B, SLC_QUERY_BLOCK, NSA_KV_HEADS, NSA_GROUP, top * SLC_BLOCK), mask)
        return jnp.einsum('bqhgn,bqhnd->bqhgd', p.astype(vg.dtype), vg)

    o_slc = sweep(slc_block, S // SLC_QUERY_BLOCK)
    k_pad = jnp.pad(k_win, ((0, 0), (WINDOW, 0), (0, 0), (0, 0)))
    v_pad = jnp.pad(v_win, ((0, 0), (WINDOW, 0), (0, 0), (0, 0)))

    def win_block(i):
        t0 = i * QUERY_BLOCK
        qb = lax.dynamic_slice_in_dim(q, t0, QUERY_BLOCK, axis=1)
        kb = lax.dynamic_slice_in_dim(k_pad, t0, WINDOW + QUERY_BLOCK, axis=1)
        vb = lax.dynamic_slice_in_dim(v_pad, t0, WINDOW + QUERY_BLOCK, axis=1)
        key_pos = t0 - WINDOW + jnp.arange(WINDOW + QUERY_BLOCK)
        tq = (t0 + jnp.arange(QUERY_BLOCK))[:, None]
        mask = (key_pos[None, :] <= tq) & (key_pos[None, :] > tq - WINDOW) & (key_pos[None, :] >= 0)
        s = jnp.einsum('bqhgd,bkhd->bhgqk', qb, kb) * scale
        p = masked_softmax(s, mask)
        return jnp.einsum('bhgqk,bkhd->bqhgd', p.astype(vb.dtype), vb)

    o_win = sweep(win_block, S // QUERY_BLOCK)
    out = gates[..., 0:1] * o_cmp + gates[..., 1:2] * o_slc + gates[..., 2:3] * o_win
    return out.reshape(B, S, NSA_WIDTH)

def diff_attention(q, k, v, lam_params, subln_g, lambda_init):
    B, S = q.shape[0], q.shape[1]
    lp = lam_params.astype(jnp.float32)
    lam = jnp.exp(jnp.sum(lp[0] * lp[1])) - jnp.exp(jnp.sum(lp[2] * lp[3])) + lambda_init
    scale = DIFF_QK_DIM ** -0.5
    kpos = jnp.arange(S)

    def block(i):
        t0 = i * QUERY_BLOCK
        qb = lax.dynamic_slice_in_dim(q, t0, QUERY_BLOCK, axis=1)
        mask = kpos[None, :] <= (t0 + jnp.arange(QUERY_BLOCK))[:, None]
        s = jnp.einsum('bqhcd,bkhcd->bhcqk', qb, k) * scale
        p = masked_softmax(s, mask)
        a = p[:, :, 0] - lam * p[:, :, 1]
        return jnp.einsum('bhqk,bkhd->bqhd', a.astype(v.dtype), v)

    o = sweep(block, S // QUERY_BLOCK).astype(jnp.float32)
    o = o * lax.rsqrt(jnp.mean(jnp.square(o), axis=-1, keepdims=True) + LN_EPS) * subln_g.astype(jnp.float32)
    o = o * (1.0 - lambda_init)
    return o.astype(v.dtype).reshape(B, S, DIFF_WIDTH)

def forgetting_attention(q, k, v, f_logit):
    B, S = q.shape[0], q.shape[1]
    c = jnp.cumsum(jax.nn.log_sigmoid(f_logit.astype(jnp.float32)), axis=1)
    cT = jnp.transpose(c, (0, 2, 1))
    scale = HEAD_DIM ** -0.5
    kpos = jnp.arange(S)

    def block(i):
        t0 = i * QUERY_BLOCK
        qb = lax.dynamic_slice_in_dim(q, t0, QUERY_BLOCK, axis=1)
        cq = lax.dynamic_slice_in_dim(cT, t0, QUERY_BLOCK, axis=2)
        mask = kpos[None, :] <= (t0 + jnp.arange(QUERY_BLOCK))[:, None]
        s = jnp.einsum('bqhd,bkhd->bhqk', qb, k).astype(jnp.float32) * scale + (cq[..., :, None] - cT[..., None, :])
        p = masked_softmax(s, mask)
        return jnp.einsum('bhqk,bkhd->bqhd', p.astype(v.dtype), v)

    return sweep(block, S // QUERY_BLOCK).reshape(B, S, FOX_WIDTH)

def hybrid_mixer(x, w_in, fox_b_f, nsa_pos_k, nsa_pos_v, nsa_phi_k1, nsa_phi_k2, nsa_phi_v1, nsa_phi_v2,
                 diff_lambda, diff_subln_g, w_out, lambda_init):
    B, S, _ = x.shape
    pos = jnp.arange(S, dtype=jnp.int32)
    proj = x @ w_in
    offsets = np.cumsum(IN_SPLITS)[:-1].tolist()
    nsa_q, nsa_kv, nsa_g, diff_q, diff_k, diff_v, fox_q, fox_k, fox_v, fox_f = jnp.split(proj, offsets, axis=-1)
    q = rope(nsa_q.reshape(B, S, NSA_HEADS, HEAD_DIM), pos).reshape(B, S, NSA_KV_HEADS, NSA_GROUP, HEAD_DIM)
    kv = nsa_kv.reshape(B, S, 6, NSA_KV_HEADS, HEAD_DIM)
    gates = jax.nn.sigmoid(nsa_g.reshape(B, S, NSA_KV_HEADS, NSA_GROUP, NSA_BRANCHES))
    o_nsa = nsa_attention(q, kv[:, :, 0], kv[:, :, 1], rope(kv[:, :, 2], pos), kv[:, :, 3],
                          rope(kv[:, :, 4], pos), kv[:, :, 5], gates,
                          nsa_pos_k, nsa_pos_v, nsa_phi_k1, nsa_phi_k2, nsa_phi_v1, nsa_phi_v2)
    dq = rope(diff_q.reshape(B, S, 2 * DIFF_HEADS, DIFF_QK_DIM), pos).reshape(B, S, DIFF_HEADS, 2, DIFF_QK_DIM)
    dk = rope(diff_k.reshape(B, S, 2 * DIFF_HEADS, DIFF_QK_DIM), pos).reshape(B, S, DIFF_HEADS, 2, DIFF_QK_DIM)
    o_diff = diff_attention(dq, dk, diff_v.reshape(B, S, DIFF_HEADS, DIFF_V_DIM), diff_lambda, diff_subln_g, lambda_init)
    o_fox = forgetting_attention(fox_q.reshape(B, S, FOX_HEADS, HEAD_DIM), fox_k.reshape(B, S, FOX_HEADS, HEAD_DIM),
                                 fox_v.reshape(B, S, FOX_HEADS, HEAD_DIM), fox_f + fox_b_f)
    return jnp.concatenate([o_nsa, o_diff, o_fox], axis=-1) @ w_out

def first_inputs(seed: int = 0) -> dict:
    key = jax.random.key(seed)
    ks = iter(jax.random.split(key, 32))
    L = DEPTH

    def nrm(shape, scale):
        return jax.random.normal(next(ks), shape, jnp.float32) * scale

    return {
        "x": nrm((BATCH, SEQ, D_MODEL), 1.0),
        "p": nrm((DEPTH, BATCH, SEQ, PLE_DIM), 1.0),
        "ln_g": 1.0 + nrm((L, 3, D_MODEL), 0.01),
        "ln_b": nrm((L, 3, D_MODEL), 0.01),
        "ffn1_w_gate": nrm((L, D_MODEL, D_FF), D_MODEL ** -0.5),
        "ffn1_w_up": nrm((L, D_MODEL, D_FF), D_MODEL ** -0.5),
        "ffn1_w_down": nrm((L, D_FF, D_MODEL), DEEPNORM_BETA * D_FF ** -0.5),
        "ffn2_w_gate": nrm((L, D_MODEL, D_FF), D_MODEL ** -0.5),
        "ffn2_w_up": nrm((L, D_MODEL, D_FF), D_MODEL ** -0.5),
        "ffn2_w_down": nrm((L, D_FF, D_MODEL), DEEPNORM_BETA * D_FF ** -0.5),
        "w_in": nrm((L, D_MODEL, IN_COLS), D_MODEL ** -0.5),
        "fox_b_f": 2.0 + nrm((L, FOX_HEADS), 0.1),
        "nsa_pos_k": nrm((L, CMP_BLOCK, HEAD_DIM), 0.02),
        "nsa_pos_v": nrm((L, CMP_BLOCK, HEAD_DIM), 0.02),
        "nsa_phi_k1": nrm((L, CMP_BLOCK * HEAD_DIM, CMP_HIDDEN), (CMP_BLOCK * HEAD_DIM) ** -0.5),
        "nsa_phi_k2": nrm((L, CMP_HIDDEN, HEAD_DIM), CMP_HIDDEN ** -0.5),
        "nsa_phi_v1": nrm((L, CMP_BLOCK * HEAD_DIM, CMP_HIDDEN), (CMP_BLOCK * HEAD_DIM) ** -0.5),
        "nsa_phi_v2": nrm((L, CMP_HIDDEN, HEAD_DIM), CMP_HIDDEN ** -0.5),
        "diff_lambda": nrm((L, 4, DIFF_QK_DIM), 0.1),
        "diff_subln_g": 1.0 + nrm((L, DIFF_V_DIM), 0.01),
        "w_out": nrm((L, MIX_WIDTH, D_MODEL), DEEPNORM_BETA * MIX_WIDTH ** -0.5),
        "ple_w_gate": nrm((L, D_MODEL, D_MODEL), D_MODEL ** -0.5),
        "ple_b_gate": nrm((L, D_MODEL), 0.01),
        "ple_w_proj": nrm((L, PLE_DIM, D_MODEL), PLE_DIM ** -0.5),
    }

def first_block(x, p, ln_g, ln_b, ffn1_w_gate, ffn1_w_up, ffn1_w_down, ffn2_w_gate, ffn2_w_up, ffn2_w_down,
              w_in, fox_b_f, nsa_pos_k, nsa_pos_v, nsa_phi_k1, nsa_phi_k2, nsa_phi_v1, nsa_phi_v2,
              diff_lambda, diff_subln_g, w_out, ple_w_gate, ple_b_gate, ple_w_proj):
    for i in range(DEPTH):
        lambda_init = 0.8 - 0.6 * math.exp(-0.3 * i)
        h = 0.5 * swiglu(x, ffn1_w_gate[i], ffn1_w_up[i], ffn1_w_down[i])
        x = layer_norm(DEEPNORM_ALPHA * x + h, ln_g[i, 0], ln_b[i, 0])
        h = hybrid_mixer(x, w_in[i], fox_b_f[i], nsa_pos_k[i], nsa_pos_v[i], nsa_phi_k1[i], nsa_phi_k2[i],
                         nsa_phi_v1[i], nsa_phi_v2[i], diff_lambda[i], diff_subln_g[i], w_out[i], lambda_init)
        x = layer_norm(DEEPNORM_ALPHA * x + h, ln_g[i, 1], ln_b[i, 1])
        h = 0.5 * swiglu(x, ffn2_w_gate[i], ffn2_w_up[i], ffn2_w_down[i])
        x = layer_norm(DEEPNORM_ALPHA * x + h, ln_g[i, 2], ln_b[i, 2])
        x = x + jax.nn.sigmoid(x @ ple_w_gate[i] + ple_b_gate[i]) * (p[i] @ ple_w_proj[i])
    return x


GRID_W = 64
CTX_LEN = 256
D_FF_2 = 2816
CONV_WIDTH = 31
CONV_PAD = (CONV_WIDTH - 1) // 2
N_Q_HEADS = 16
N_KV_HEADS = 4
WINDOW_2 = 128
BLOCK = 128
ROPE_BASE = 10000.0
NORM_EPS = 1e-6
N_MOD = 9
N_CONV_LAYERS = (DEPTH + 1) // 2
N_ATTN_LAYERS = DEPTH // 2
Q_DIM = N_Q_HEADS * HEAD_DIM
KV_DIM = N_KV_HEADS * HEAD_DIM


def rmsnorm(x, g):
    xf = x.astype(jnp.float32)
    y = xf * lax.rsqrt(jnp.mean(xf * xf, axis=-1, keepdims=True) + NORM_EPS)
    return y.astype(x.dtype) * g

def modulate(x, g, shift, scale):
    return rmsnorm(x, g) * (1 + scale) + shift

def swiglu_2(h, w_in, w_out):
    gu = h @ w_in
    gate, up = jnp.split(gu, 2, axis=-1)
    return (jax.nn.silu(gate) * up) @ w_out

def conformer_conv(h, pw1_w, pw1_b, dw_w, dw_b, ln_g, ln_b, pw2_w, pw2_b):
    a = h @ pw1_w + pw1_b
    u, g = jnp.split(a, 2, axis=-1)
    u = u * jax.nn.sigmoid(g)
    u = lax.conv_general_dilated(
        u, dw_w[:, None, :].astype(u.dtype), window_strides=(1,),
        padding=[(CONV_PAD, CONV_PAD)], dimension_numbers=("NWC", "WIO", "NWC"),
        feature_group_count=D_MODEL) + dw_b
    uf = u.astype(jnp.float32)
    mu = jnp.mean(uf, axis=-1, keepdims=True)
    var = jnp.mean(jnp.square(uf - mu), axis=-1, keepdims=True)
    u = ((uf - mu) * lax.rsqrt(var + NORM_EPS)).astype(u.dtype) * ln_g + ln_b
    return jax.nn.silu(u) @ pw2_w + pw2_b

def axial_rope_tables(n_tok):
    n_rows = n_tok // GRID_W
    row = jnp.repeat(jnp.arange(n_rows), GRID_W).astype(jnp.float32)
    col = jnp.tile(jnp.arange(GRID_W), n_rows).astype(jnp.float32)
    n_freq = HEAD_DIM // 4
    inv = ROPE_BASE ** (-jnp.arange(n_freq, dtype=jnp.float32) / n_freq)
    ang = jnp.stack([row[:, None] * inv, col[:, None] * inv], axis=1)
    return jnp.cos(ang), jnp.sin(ang)

def apply_rope(x, cos, sin):
    n_freq = HEAD_DIM // 4
    xs = x.reshape(x.shape[:-1] + (2, 2, n_freq))
    x1 = xs[..., 0, :]
    x2 = xs[..., 1, :]
    bshape = (1, cos.shape[0]) + (1,) * (x.ndim - 3) + (2, n_freq)
    cs = cos.reshape(bshape).astype(x.dtype)
    sn = sin.reshape(bshape).astype(x.dtype)
    out = jnp.stack([x1 * cs - x2 * sn, x1 * sn + x2 * cs], axis=-2)
    return out.reshape(x.shape)

def windowed_gqa_sink(h_lat, h_ctx, w_qkv, w_o, sink, with_ctx_out):
    B, S, _ = h_lat.shape
    C = h_ctx.shape[1]
    G = N_Q_HEADS // N_KV_HEADS
    scale = HEAD_DIM ** -0.5

    def proj(h):
        qkv = h @ w_qkv
        q = qkv[..., :Q_DIM].reshape(h.shape[:2] + (N_KV_HEADS, G, HEAD_DIM))
        k = qkv[..., Q_DIM:Q_DIM + KV_DIM].reshape(h.shape[:2] + (N_KV_HEADS, HEAD_DIM))
        v = qkv[..., Q_DIM + KV_DIM:].reshape(h.shape[:2] + (N_KV_HEADS, HEAD_DIM))
        return q, k, v

    ql, kl, vl = proj(h_lat)
    qc, kc, vc = proj(h_ctx)
    cos, sin = axial_rope_tables(S)
    ql = apply_rope(ql, cos, sin) * scale
    kl = apply_rope(kl, cos, sin)
    pad = ((0, 0), (WINDOW_2, WINDOW_2), (0, 0), (0, 0))
    k_pad = jnp.pad(kl, pad)
    v_pad = jnp.pad(vl, pad)
    sink_col = sink.reshape(N_KV_HEADS, G, 1, 1).astype(jnp.float32)
    kw = BLOCK + 2 * WINDOW_2

    def one_block(n):
        start = n * BLOCK
        qb = lax.dynamic_slice_in_dim(ql, start, BLOCK, axis=1)
        kb = lax.dynamic_slice_in_dim(k_pad, start, kw, axis=1)
        vb = lax.dynamic_slice_in_dim(v_pad, start, kw, axis=1)
        i_pos = start + jnp.arange(BLOCK)
        j_pos = start - WINDOW_2 + jnp.arange(kw)
        valid = ((jnp.abs(j_pos[None, :] - i_pos[:, None]) <= WINDOW_2)
                 & (j_pos[None, :] >= 0) & (j_pos[None, :] < S))
        s_win = jnp.einsum('bqhgd,bkhd->bhgqk', qb, kb).astype(jnp.float32)
        s_win = jnp.where(valid, s_win, -jnp.inf)
        s_ctx = jnp.einsum('bqhgd,bchd->bhgqc', qb, kc).astype(jnp.float32)
        sinks = jnp.broadcast_to(sink_col, s_win.shape[:-1] + (1,))
        p = jax.nn.softmax(jnp.concatenate([s_win, s_ctx, sinks], axis=-1), axis=-1).astype(vb.dtype)
        o = (jnp.einsum('bhgqk,bkhd->bqhgd', p[..., :kw], vb)
             + jnp.einsum('bhgqc,bchd->bqhgd', p[..., kw:kw + C], vc))
        return o.reshape(B, BLOCK, Q_DIM)

    o = lax.map(one_block, jnp.arange(S // BLOCK))
    y_lat = jnp.moveaxis(o, 0, 1).reshape(B, S, Q_DIM) @ w_o

    y_ctx = None
    if with_ctx_out:
        s = jnp.einsum('bqhgd,bkhd->bhgqk', qc * scale, kc).astype(jnp.float32)
        sinks = jnp.broadcast_to(sink_col, s.shape[:-1] + (1,))
        p = jax.nn.softmax(jnp.concatenate([s, sinks], axis=-1), axis=-1).astype(vc.dtype)
        oc = jnp.einsum('bhgqk,bkhd->bqhgd', p[..., :C], vc)
        y_ctx = oc.reshape(B, C, Q_DIM) @ w_o
    return y_lat, y_ctx

def second_inputs(seed: int = 0) -> dict:
    key = jax.random.key(seed)
    ks = jax.random.split(key, 32)
    f32 = jnp.float32

    def nrm(k, shape, s):
        return jax.random.normal(k, shape, f32) * s

    D, F = D_MODEL, D_FF_2
    NC, NA = N_CONV_LAYERS, N_ATTN_LAYERS
    return {
        "x": nrm(ks[0], (BATCH, SEQ, D), 1.0),
        "c": nrm(ks[1], (BATCH, D), 1.0),
        "ctx": nrm(ks[2], (BATCH, CTX_LEN, D), 1.0),
        "c_ctx": nrm(ks[3], (D,), 1.0),
        "norm_g": 1.0 + nrm(ks[4], (DEPTH, 3, D), 0.05),
        "ada_w": nrm(ks[5], (DEPTH, D, N_MOD * D), D ** -0.5),
        "ada_b": nrm(ks[6], (DEPTH, N_MOD * D), 0.02),
        "ffn1_wi": nrm(ks[7], (DEPTH, D, 2 * F), D ** -0.5),
        "ffn1_wo": nrm(ks[8], (DEPTH, F, D), F ** -0.5),
        "ffn2_wi": nrm(ks[9], (DEPTH, D, 2 * F), D ** -0.5),
        "ffn2_wo": nrm(ks[10], (DEPTH, F, D), F ** -0.5),
        "conv_pw1_w": nrm(ks[11], (NC, D, 2 * D), D ** -0.5),
        "conv_pw1_b": nrm(ks[12], (NC, 2 * D), 0.02),
        "conv_dw_w": nrm(ks[13], (NC, CONV_WIDTH, D), CONV_WIDTH ** -0.5),
        "conv_dw_b": nrm(ks[14], (NC, D), 0.02),
        "conv_ln_g": 1.0 + nrm(ks[15], (NC, D), 0.05),
        "conv_ln_b": nrm(ks[16], (NC, D), 0.02),
        "conv_pw2_w": nrm(ks[17], (NC, D, D), D ** -0.5),
        "conv_pw2_b": nrm(ks[18], (NC, D), 0.02),
        "attn_w_qkv": nrm(ks[19], (NA, D, Q_DIM + 2 * KV_DIM), D ** -0.5),
        "attn_w_o": nrm(ks[20], (NA, Q_DIM, D), Q_DIM ** -0.5),
        "attn_sink": nrm(ks[21], (NA, N_Q_HEADS), 1.0),
        "final_g": 1.0 + nrm(ks[22], (D,), 0.05),
    }

def second_block(x, c, ctx, c_ctx, norm_g, ada_w, ada_b, ffn1_wi, ffn1_wo, ffn2_wi, ffn2_wo,
              conv_pw1_w, conv_pw1_b, conv_dw_w, conv_dw_b, conv_ln_g, conv_ln_b,
              conv_pw2_w, conv_pw2_b, attn_w_qkv, attn_w_o, attn_sink, final_g):
    for i in range(DEPTH):
        last = i == DEPTH - 1
        m_lat = (jax.nn.silu(c) @ ada_w[i] + ada_b[i])[:, None, :]
        m_ctx = (jax.nn.silu(c_ctx) @ ada_w[i] + ada_b[i])[None, None, :]
        sh1, sc1, gt1, sh2, sc2, gt2, sh3, sc3, gt3 = jnp.split(m_lat, N_MOD, axis=-1)
        ch1, cs1, cg1, ch2, cs2, cg2, ch3, cs3, cg3 = jnp.split(m_ctx, N_MOD, axis=-1)
        g1, g2, g3 = norm_g[i, 0], norm_g[i, 1], norm_g[i, 2]

        x = x + 0.5 * gt1 * swiglu_2(modulate(x, g1, sh1, sc1), ffn1_wi[i], ffn1_wo[i])
        ctx = ctx + 0.5 * cg1 * swiglu_2(modulate(ctx, g1, ch1, cs1), ffn1_wi[i], ffn1_wo[i])

        hx = modulate(x, g2, sh2, sc2)
        hc = modulate(ctx, g2, ch2, cs2)
        j = i // 2
        if i % 2 == 0:
            conv_args = (conv_pw1_w[j], conv_pw1_b[j], conv_dw_w[j], conv_dw_b[j],
                         conv_ln_g[j], conv_ln_b[j], conv_pw2_w[j], conv_pw2_b[j])
            y_lat = conformer_conv(hx, *conv_args)
            y_ctx = None if last else conformer_conv(hc, *conv_args)
        else:
            y_lat, y_ctx = windowed_gqa_sink(hx, hc, attn_w_qkv[j], attn_w_o[j],
                                             attn_sink[j], not last)
        x = x + gt2 * y_lat

        x = x + 0.5 * gt3 * swiglu_2(modulate(x, g3, sh3, sc3), ffn2_wi[i], ffn2_wo[i])
        if not last:
            ctx = ctx + cg2 * y_ctx
            ctx = ctx + 0.5 * cg3 * swiglu_2(modulate(ctx, g3, ch3, cs3), ffn2_wi[i], ffn2_wo[i])
    return rmsnorm(x, final_g)


def setup_inputs(seed=0):
    out = dict(first_inputs(seed))
    for name, value in second_inputs(seed + 1).items():
        if name != "x":
            out[name + "_2"] = value
    return out


def reference(
    x, p, ln_g, ln_b, ffn1_w_gate, ffn1_w_up, ffn1_w_down, ffn2_w_gate, ffn2_w_up, ffn2_w_down,
    w_in, fox_b_f, nsa_pos_k, nsa_pos_v, nsa_phi_k1, nsa_phi_k2, nsa_phi_v1, nsa_phi_v2,
    diff_lambda, diff_subln_g, w_out, ple_w_gate, ple_b_gate, ple_w_proj, c_2, ctx_2, c_ctx_2,
    norm_g_2, ada_w_2, ada_b_2, ffn1_wi_2, ffn1_wo_2, ffn2_wi_2, ffn2_wo_2, conv_pw1_w_2,
    conv_pw1_b_2, conv_dw_w_2, conv_dw_b_2, conv_ln_g_2, conv_ln_b_2, conv_pw2_w_2,
    conv_pw2_b_2, attn_w_qkv_2, attn_w_o_2, attn_sink_2, final_g_2,
):
    x = first_block(
        x, p, ln_g, ln_b, ffn1_w_gate, ffn1_w_up, ffn1_w_down, ffn2_w_gate, ffn2_w_up,
        ffn2_w_down, w_in, fox_b_f, nsa_pos_k, nsa_pos_v, nsa_phi_k1, nsa_phi_k2, nsa_phi_v1,
        nsa_phi_v2, diff_lambda, diff_subln_g, w_out, ple_w_gate, ple_b_gate, ple_w_proj,
    )
    return second_block(
        x, c_2, ctx_2, c_ctx_2, norm_g_2, ada_w_2, ada_b_2, ffn1_wi_2, ffn1_wo_2, ffn2_wi_2,
        ffn2_wo_2, conv_pw1_w_2, conv_pw1_b_2, conv_dw_w_2, conv_dw_b_2, conv_ln_g_2,
        conv_ln_b_2, conv_pw2_w_2, conv_pw2_b_2, attn_w_qkv_2, attn_w_o_2, attn_sink_2,
        final_g_2,
    )


_drawn_inputs = setup_inputs


def setup_inputs(seed=0):
    import zlib

    import numpy as np

    out = dict(_drawn_inputs(seed))
    spreads = {}
    factors = {'fox_b_f': 51.448,
     'nsa_pos_k': 200.0,
     'nsa_pos_v': 200.0,
     'nsa_phi_k1': 28.798,
     'nsa_phi_k2': 28.361,
     'diff_lambda': 5.678,
     'diff_subln_g': 176.418,
     'ple_b_gate': 22.853,
     'conv_pw1_b_2': 8.0,
     'conv_dw_b_2': 6.09,
     'conv_ln_g_2': 3.005,
     'conv_ln_b_2': 8.0,
     'conv_pw2_b_2': 5.129,
     'attn_sink_2': 8.0,
     'nsa_phi_v1': 3.256,
     'nsa_phi_v2': 2.95}
    for name, (base, spread) in spreads.items():
        noise = np.random.default_rng([zlib.crc32(name.encode()), seed]).standard_normal(out[name].shape)
        drawn = base * np.exp(spread * noise) if base else spread * noise
        out[name] = __import__('jax').numpy.asarray(drawn.astype(out[name].dtype))
    for name, factor in factors.items():
        out[name] = (out[name] * factor).astype(out[name].dtype)
    return out
```

```python
import math
from contextlib import ExitStack

import numpy as np

import concourse.bass as bass
from concourse import mybir

P = 128
D = 1024
KT = D // P
S = 256
ST = S // P
DEPTH = 2
FF = 2816
FT = FF // P
UNIT = 2048
RING = 11
LOOPS = 2
NEG = -1e30
ALPHA = (2.0 * DEPTH) ** 0.25
CMP_BLOCK, CMP_STRIDE = 32, 16
NC = (S - CMP_BLOCK) // CMP_STRIDE + 1
HID = 256
TAPS = 31
PAD = (TAPS - 1) // 2
NMOD = 9
PITCH = 32

F32 = mybir.dt.float32
ALU = mybir.AluOpType
ACT = mybir.ActivationFunctionType
AX = mybir.AxisListType

(T_CMP, T_KSLC, T_KWIN, T_FORGET, T_NQ, T_DQ, T_DK, T_FQ, T_FK) = (0, 1, 2, 3, 4, 6, 8, 10, 14)
PROJ_SCALE = [1.0, 1.0, 64 ** -0.5, 32 ** -0.5, 1.0, 64 ** -0.5, 64 ** -0.5, 1.0, 1.0]
V_SLC, V_WIN, V_DIFF, V_FOX, V_ALL = 0, 64, 128, 384, 896


def columns():
    widths = [("ident", P), ("swap64", P), ("swap32", P), ("swapax", P), ("mean", P), ("low", P), ("high", P),
              ("nsa_cos", S), ("nsa_sin", S), ("diff_cos", S), ("diff_sin", S), ("ax_cos", S), ("ax_sin", S),
              ("cmp_add", ST * NC), ("cmp_mul", ST * NC), ("kc_cos", NC), ("kc_sin", NC),
              ("eps", 4), ("csil", KT * 2), ("final_g", KT), ("sink", 16), ("conv_w", KT * TAPS),
              ("conv_b", KT), ("conv_ln_g", KT), ("conv_ln_b", KT), ("pw1_b", 2 * KT), ("pw2_b", KT)]
    for l in range(DEPTH):
        widths += [(f"ln_g{l}", 3 * KT), (f"ln_b{l}", 3 * KT), (f"ple_b{l}", KT), (f"pos{l}", CMP_BLOCK),
                   (f"fox_b{l}", 1), (f"lam{l}", 4 * 32), (f"subln{l}", 64),
                   (f"ada_b{l}", NMOD * KT), (f"norm_g{l}", 3 * KT)]
    at, place = 0, {}
    for name, w in widths:
        place[name] = (at, w)
        at += w
    return place, at


def lay_constants(inp):
    place, width = columns()
    c = np.zeros((P, width), np.float32)

    def put(name, a, rows=slice(0, P)):
        s, w = place[name]
        c[rows, s:s + w] = a

    p = np.arange(P)
    put("ident", np.eye(P, dtype=np.float32))
    for name, block in (("swap64", 64), ("swap32", 32), ("swapax", 32)):
        m = np.zeros((P, P), np.float32)
        other = (p // block) * block + (p % block + block // 2) % block
        m[other, p] = 1.0
        put(name, m)
    put("mean", 1.0 / D)
    put("low", np.where(p[None, :] <= p[:, None], 0.0, NEG))
    put("high", np.where(p[None, :] >= p[:, None], 0.0, NEG))

    def rope_tables(name, dim, pos):
        inv = (np.float32(10000.0) ** (-np.arange(0, dim, 2, dtype=np.float32) / np.float32(dim))).astype(np.float32)
        ang = pos.astype(np.float32)[None, :] * inv[p % (dim // 2)][:, None]
        sign = np.where(p % dim < dim // 2, -1.0, 1.0)[:, None]
        put(f"{name}_cos", np.cos(ang))
        put(f"{name}_sin", np.sin(ang) * sign)

    rope_tables("nsa", 64, np.arange(S))
    rope_tables("diff", 32, np.arange(S))
    ends = np.arange(NC) * CMP_STRIDE + CMP_BLOCK - 1
    rope_tables("kc", 64, ends)
    inv = (np.float32(10000.0) ** (-np.arange(16, dtype=np.float32) / np.float32(16))).astype(np.float32)
    t = np.arange(S)
    where = np.where((p % 64 < 32)[:, None], (t // 64)[None, :], (t % 64)[None, :]).astype(np.float32)
    ang = where * inv[p % 16][:, None]
    put("ax_cos", np.cos(ang))
    put("ax_sin", np.sin(ang) * np.where(p % 32 < 16, -1.0, 1.0)[:, None])
    seen = (ends[None, None, :] <= np.arange(S).reshape(ST, P).T[:, :, None])
    put("cmp_add", np.where(seen, 0.0, NEG).reshape(P, ST * NC))
    put("cmp_mul", np.where(seen, 1.0, 0.0).reshape(P, ST * NC))
    put("eps", np.array([4e-5, 1e-5, 1e-6, 1.0], np.float32))

    def cols(a):
        return a.reshape(-1, P).T

    put("csil", np.stack([cols(inp["c_2"]), cols(inp["c_ctx_2"])], -1).reshape(P, KT * 2))
    put("final_g", cols(inp["final_g_2"]))
    put("sink", np.broadcast_to(inp["attn_sink_2"].reshape(1, 16), (P, 16)))
    put("conv_w", inp["conv_dw_w_2"][0].reshape(TAPS, KT, P).transpose(2, 1, 0).reshape(P, KT * TAPS))
    put("conv_b", cols(inp["conv_dw_b_2"][0]))
    put("conv_ln_g", cols(inp["conv_ln_g_2"][0]))
    put("conv_ln_b", cols(inp["conv_ln_b_2"][0]))
    put("pw1_b", cols(inp["conv_pw1_b_2"][0]))
    put("pw2_b", cols(inp["conv_pw2_b_2"][0]))
    for l in range(DEPTH):
        put(f"ln_g{l}", cols(inp["ln_g"][l]))
        put(f"ln_b{l}", cols(inp["ln_b"][l]))
        put(f"ple_b{l}", cols(inp["ple_b_gate"][l]))
        put(f"pos{l}", inp["nsa_pos_k"][l].T, slice(0, 64))
        put(f"pos{l}", inp["nsa_pos_v"][l].T, slice(64, 128))
        put(f"fox_b{l}", inp["fox_b_f"][l][:, None], slice(0, 8))
        put(f"lam{l}", np.broadcast_to(inp["diff_lambda"][l].reshape(1, 128), (P, 128)))
        put(f"subln{l}", np.broadcast_to(inp["diff_subln_g"][l][None], (P, 64)))
        put(f"ada_b{l}", cols(inp["ada_b_2"][l]))
        put(f"norm_g{l}", cols(inp["norm_g_2"][l]))
    return c


def by_k(w):
    return w.reshape(-1, P, w.shape[1]).transpose(1, 0, 2)


def lay_weights(inp):
    units = []

    def unit(*parts):
        u = np.zeros((P, UNIT), np.float32)
        at = 0
        for a in parts:
            a = a.reshape(P, -1)
            u[:, at:at + a.shape[1]] = a
            at += a.shape[1]
        units.append(u)

    def ffn(gate, up, down):
        f = gate.shape[1]
        g, u = (np.zeros((D, FF), np.float32) for _ in range(2))
        d = np.zeros((FF, D), np.float32)
        g[:, :f], u[:, :f], d[:f] = gate, up, down
        g, u, d = by_k(g), by_k(u), by_k(d)
        for t in range(FT):
            unit(g[:, :, t * P:t * P + P], u[:, :, t * P:t * P + P])
        for t in range(0, FT, 2):
            unit(d[:, t:t + 2])

    def pairs(w):
        w = by_k(w)
        for n in range(0, w.shape[2], 2 * P):
            unit(w[:, :, n:n + 2 * P])

    def mixer(l):
        w = inp["w_in"][l]
        split = np.cumsum([256, 384, 12, 256, 256, 256, 512, 512, 512, 8])
        nq, nkv, gates, dq, dk, dv, fq, fk, fv, ff = np.split(w, split[:-1], axis=1)
        kv = [nkv[:, 64 * n:64 * n + 64] for n in range(6)]
        last = np.zeros((D, P), np.float32)
        last[:, 0:8], last[:, 32:44] = ff, gates
        pairs(np.concatenate([kv[0], kv[1], kv[2], kv[2], kv[4], kv[4], last, nq, dq, dk, fq, fk], axis=1))
        v = by_k(np.concatenate([kv[3], kv[5], dv, fv], axis=1))
        for n in range(3):
            unit(v[:, :, 256 * n:256 * n + 256])
        one = np.concatenate([inp[n][l].reshape(CMP_BLOCK, 64, HID).transpose(1, 0, 2)
                              for n in ("nsa_phi_k1", "nsa_phi_v1")], axis=0)
        for n in range(4):
            unit(one[:, 8 * n:8 * n + 8])
        k2, v2 = by_k(inp["nsa_phi_k2"][l]), by_k(inp["nsa_phi_v2"][l])
        unit(v[:, :, 768:896], np.concatenate([k2, k2], axis=2), v2)
        pairs(inp["w_out"][l])

    for l in range(DEPTH):
        ffn(inp["ffn1_w_gate"][l], inp["ffn1_w_up"][l], inp["ffn1_w_down"][l])
        mixer(l)
        ffn(inp["ffn2_w_gate"][l], inp["ffn2_w_up"][l], inp["ffn2_w_down"][l])
        pairs(inp["ple_w_gate"][l])
        unit(by_k(inp["ple_w_proj"][l]))
    for l in range(DEPTH):
        pairs(inp["ada_w_2"][l])
        w = inp["ffn1_wi_2"][l]
        ffn(w[:, :FF], w[:, FF:], inp["ffn1_wo_2"][l])
        if l == 0:
            w = by_k(inp["conv_pw1_w_2"][0])
            for t in range(KT):
                unit(w[:, :, t * P:t * P + P], w[:, :, D + t * P:D + t * P + P])
            pairs(inp["conv_pw2_w_2"][0])
        else:
            w = inp["attn_w_qkv_2"][0]
            q = w[:, :D].reshape(D, 2, 2, 4, 64).transpose(0, 1, 3, 2, 4).reshape(D, D)
            pairs(np.concatenate([q, w[:, D:D + 256]], axis=1))
            unit(by_k(w[:, D + 256:D + 512]))
            pairs(inp["attn_w_o_2"][0])
        w = inp["ffn2_wi_2"][l]
        ffn(w[:, :FF], w[:, FF:], inp["ffn2_wo_2"][l])
    return np.stack(units)


def lay_rows(x):
    return np.ascontiguousarray(x[0].T.reshape(KT, P, S).transpose(1, 0, 2))


class Seen:

    def __init__(self):
        self.at = {}

    def __call__(self, sem, n=1):
        self.at[sem.name] = self.at.get(sem.name, 0) + n
        return self.at[sem.name]

    def now(self, sem):
        return self.at.get(sem.name, 0)


def build(nc, weights, consts, x_in, ctx_in, p_in, out, n_units):
    place, width = columns()
    with ExitStack() as stack:
        def sb(name, shape, dt=F32):
            return stack.enter_context(nc.sbuf_tensor(name, shape, dt))

        def sem(name):
            return stack.enter_context(nc.semaphore(name))

        ps = stack.enter_context(nc.psum_tensor("ps", [P, 8, 512], F32))
        ring = sb("ring", [P, RING, UNIT])
        hidden = sb("hidden", [P, FT, 512])
        x = sb("x", [P, KT, 512])
        z = sb("z", [P, KT, 512])
        cst = sb("cst", [P, width])
        ple_p = sb("ple_p", [P, DEPTH, 2, S])
        gated = sb("gated", [P, 2, 512])
        std = sb("std", [P, 512])
        rstd = sb("rstd", [P, 512])
        mods = sb("mods", [P, NMOD, KT, 2])
        mod_a = sb("mod_a", [P, 3, KT, 2])
        cs = sb("cs", [P, KT, 2])
        block_kv = sb("block_kv", [P, CMP_BLOCK, 2 * NC])
        hid = sb("hid", [P, 2, 2 * NC])
        hid4 = sb("hid4", [P, 2, 4, PITCH])
        kc = sb("kc", [P, NC])
        kc_t = sb("kc_t", [P, NC])
        vc_diag = sb("vc_diag", [P, 4 * 64])
        sc = sb("sc", [P, ST, 4, PITCH])
        pc_t = sb("pc_t", [P, ST, P])
        cmp_m = sb("cmp_m", [P, 8])
        cmp_s = sb("cmp_s", [P, 8])
        gates = sb("gates", [P, ST, 12])
        fl = sb("fl", [8, 4, S])
        forget = sb("forget", [8, S])
        lam_t = sb("lam_t", [P, 64])
        lam_s = sb("lam_s", [P, 4])
        subg = sb("subg", [P, 64])
        neg_max = sb("neg_max", [P, 32, 2])
        sums = sb("sums", [P, 32, 2])
        coef = sb("coef", [P, 32, 2])
        sink_e = sb("sink_e", [P, 32])
        rms = sb("rms", [P, 8])
        flat = hidden[:].rearrange("p a b -> p (a b)")

        def carve(start, *shape):
            n = int(np.prod(shape))
            names = " ".join("abcd"[:len(shape)])
            return flat[:, start:start + n].rearrange(f"p ({names}) -> p {names}", **dict(zip("abcd", shape)))

        proj = carve(0, 18, S)
        val = carve(4608, ST, V_ALL)
        probs = carve(6400, 3, 512)
        probs_t = carve(7936, 2, 512)
        heads = carve(8960, ST, D)
        part = carve(0, ST, 512)
        tmp = gated
        square = hidden
        conv_in = carve(0, KT, 2, S + 2 * PAD)
        conv_out = z
        q_at = carve(0, KT, S)
        k_at = carve(2048, 2, 512)
        v_at = carve(3072, 4, 256)
        probs2 = carve(6400, 3, 512)

        def c(name, rows=slice(0, P)):
            s, w = place[name]
            return cst[rows, s:s + w]

        landed = [sem(f"unit_landed{i}") for i in range(RING)]
        params_landed = sem("params_landed")
        unit_done = sem("unit_done")
        silu_ready = sem("silu_ready")
        hidden_ready = sem("hidden_ready")
        z_ready = sem("z_ready")
        stat_ready = sem("stat_ready")
        dev_ready = sem("dev_ready")
        sq_ready = sem("sq_ready")
        std_ready = sem("std_ready")
        scaled_ready = sem("scaled_ready")
        norm_ready = sem("norm_ready")
        sig_ready = sem("sig_ready")
        res_ready = sem("res_ready")
        dve_step = sem("dve_step")
        act_step = sem("act_step")
        stored = sem("stored")
        memsets = sem("memsets")
        proj_ready = sem("proj_ready")
        val_ready = sem("val_ready")
        gate_sum = sem("gate_sum")
        gates_ready = sem("gates_ready")
        swapped = sem("swapped")
        rope_ready = sem("rope_ready")
        blocks_ready = sem("blocks_ready")
        gelu_ready = sem("gelu_ready")
        hid4_ready = sem("hid4_ready")
        kc_sum = sem("kc_sum")
        kc_raw = sem("kc_raw")
        kc_swapped = sem("kc_swapped")
        kc_ready = sem("kc_ready")
        forget_in = sem("forget_in")
        forget_act = sem("forget_act")
        forget_ready = sem("forget_ready")
        lam_in = sem("lam_in")
        lam_act = sem("lam_act")
        cmp_scores = sem("cmp_scores")
        cmp_in = sem("cmp_in")
        cmp_exp = sem("cmp_exp")
        cmp_probs = sem("cmp_probs")
        cmp_turned = sem("cmp_turned")
        cmp_t = sem("cmp_t")
        cmp_out = sem("cmp_out")
        score_ready = sem("score_ready")
        max_ready = sem("max_ready")
        exp_done = sem("exp_done")
        turned = sem("turned")
        probs_t_ready = sem("probs_t_ready")
        out_ready = sem("out_ready")
        out_taken = sem("out_taken")
        rms_in = sem("rms_in")
        rms_act = sem("rms_act")
        heads_turned = sem("heads_turned")
        heads_ready = sem("heads_ready")
        mods_ready = sem("mods_ready")
        cs_ready = sem("cs_ready")
        conv_ready = sem("conv_ready")

        block = stack.enter_context(nc.Block())

        def stages(e):
            e.start()
            for l in range(DEPTH):
                e.ffn(S, x, e.x_from_prev, 2)
                e.post_norm(2 * ALPHA, 0, c(f"ln_g{l}")[:, 0:KT], c(f"ln_b{l}")[:, 0:KT])
                e.mixer(l)
                e.post_norm(ALPHA, 1, c(f"ln_g{l}")[:, KT:2 * KT], c(f"ln_b{l}")[:, KT:2 * KT])
                e.ffn(S, x, e.x_from_norm, 1)
                e.post_norm(2 * ALPHA, 0, c(f"ln_g{l}")[:, 2 * KT:3 * KT], c(f"ln_b{l}")[:, 2 * KT:3 * KT])
                e.ple(l)
            for l in range(DEPTH):
                e.ada(l)
                e.pre_norm(512, 0)
                e.ffn(512, z, e.x_from_norm, 2)
                e.residual(512, 2)
                e.pre_norm(512, 1)
                if l == 0:
                    e.conv()
                    e.residual(512, 5)
                else:
                    e.attention()
                    e.residual(S, 5)
                T = 512 if l == 0 else S
                e.pre_norm(T, 2)
                e.ffn(T, z, e.x_from_norm, 2)
                e.residual(T, 8)
            e.finish()

        def y_tile(T, d):
            return ps[:, d, :] if T == 512 else ps[:, 4 + d // 2, d % 2 * S:d % 2 * S + S]

        def y_bank(b):
            return ps[:, 4 + b, :].rearrange("p (t s) -> p t s", t=2)

        def halves(T):
            return [slice(i, i + S) for i in range(0, T, S)]

        def mixer_jobs():
            jobs = []
            for t in range(ST):
                for i in range(4):
                    maps = [(T_DQ + n, T_DK + n, 32 * i, 32, V_DIFF + 64 * (2 * n + i // 2), None) for n in range(2)]
                    jobs.append((t, maps, "diff0" if i % 2 == 0 else "diff1", 256 + 64 * (i // 2)))
                for kind, kt, vc in (("slc", T_KSLC, V_SLC), ("win", T_KWIN, V_WIN)):
                    for i in range(2):
                        maps = [(T_NQ + n, kt, 64 * i, 64, vc, None) for n in range(2)]
                        jobs.append((t, maps, kind, 64 * i))
                for m in range(2):
                    for i in range(2):
                        maps = [(T_FQ + 2 * m + n, T_FK + 2 * m + n, 64 * i, 64, V_FOX + 64 * (4 * m + 2 * n + i),
                                 4 * m + 2 * n + i) for n in range(2)]
                        jobs.append((t, maps, "fox", 512 + 64 * (4 * m + i)))
            return jobs

        JOBS = mixer_jobs()
        JOBS2 = [(t, p, g, i) for t in range(ST) for p in range(2) for g in range(4) for i in range(2)]

        @block.sync
        def _(sp):
            sp.dma_start(x[:, :, 0:S], x_in).then_inc(params_landed, 16)
            sp.dma_start(cst[:], consts).then_inc(params_landed, 16)
            whole = n_units // RING
            for n in range(RING):
                sp.dma_start(ring[:, n, :], weights[n]).then_inc(landed[n], 16)
            sp.dma_start(ple_p[:], p_in).then_inc(params_landed, 16)
            sp.dma_start(x[:, :, S:512], ctx_in).then_inc(params_landed, 16)
            with sp.Fori(1, whole) as lap:
                for n in range(RING):
                    sp.wait_ge(unit_done, (lap - 1) * RING + (n + 1))
                    sp.dma_start(ring[:, n, :], weights[lap * RING + n]).then_inc(landed[n], 16)
            for n in range(n_units % RING):
                sp.wait_ge(unit_done, (whole - 1) * RING + n + 1)
                sp.dma_start(ring[:, n, :], weights[whole * RING + n]).then_inc(landed[n], 16)

        class Engine:
            pass

        class PE(Engine):
            def __init__(self, pe):
                self.pe, self.seen, self.u = pe, Seen(), 0

            def start(self):
                self.hid_base = RING
                self.pe.wait_ge(params_landed, 64)

            def x_from_prev(self, k):
                if self.u > 0 and k % 2 == 0:
                    self.pe.wait_ge(res_ready, self.seen(res_ready))

            def x_from_norm(self, k, per=1):
                self.pe.wait_ge(norm_ready, self.seen(norm_ready, per))

            def unit(self):
                s = self.u % RING
                self.pe.wait_ge(landed[s], 16 * (self.u // RING + 1))
                return ring[:, s, :]

            def done(self, mm):
                mm.then_inc(unit_done, 1)
                self.u += 1

            def mm(self, out, lhsT, rhs, first, last, **kw):
                return nc.tensor.matmul(out, lhsT, rhs, start=first, stop=last, **kw)

            def ffn(self, T, xin, x_from, x_per):
                pe, u0, h0 = self.pe, self.u, self.hid_base
                per = 2 if T == 512 and x_from == self.x_from_norm else 1
                if x_from == self.x_from_norm:
                    for k in range(KT):
                        x_from(k, per)
                else:
                    for k in range(KT):
                        x_from(k)
                ways = 2 if T == 512 else 4
                with pe.Fori(0, LOOPS) as i:
                    for j in range(RING):
                        slot = (u0 + j) % RING
                        pe.wait_ge(landed[slot], i * 16 + 16 * ((u0 + j) // RING + 1))
                        prev = j - ways if j >= ways else max(n for n in range(RING) if n % ways == j) - RING
                        pe.wait_ge(hidden_ready, i * RING + (h0 + prev + 1))
                        w = ring[:, slot, :].rearrange("p (g k m) -> p g k m", g=2, k=KT)
                        for g in range(2):
                            o = ps[:, 2 * (j % 2) + g, :] if T == 512 else ps[:, j % 4, g * S:g * S + S]
                            for k in range(KT):
                                m = self.mm(o, w[:, g, k, :], xin[:, k, 0:T], k == 0, k == KT - 1)
                        m.then_inc(unit_done, 1)
                self.u += FT
                self.hid_base += FT
                for n in range(FT // 2):
                    w = self.unit().rearrange("p (f d) -> p f d", f=2)
                    pe.wait_ge(hidden_ready, h0 + (FT if T == 512 else 2 * n + 2))
                    for f in range(2):
                        for d in range(KT):
                            first = n == 0 and f == 0 and (T == 512 or d % 2 == 0)
                            m = self.mm(y_tile(T, d), w[:, f, d * P:d * P + P], hidden[:, 2 * n + f, 0:T],
                                        first, n == FT // 2 - 1 and f == 1, skip_group_check=True)
                    self.done(m)

            def stats(self, T, bank, ready, per, src):
                for k in range(KT):
                    if k % 2 == 0:
                        self.pe.wait_ge(ready, self.seen(ready, per))
                    m = self.mm(ps[:, bank, 0:T], c("mean"), src[:, k, 0:T], k == 0, k == KT - 1)
                m.then_inc(stat_ready, 1)

            def post_norm(self, scale, eps, g, b):
                self.stats(S, 0, z_ready, 1, z)
                self.stats(S, 1, sq_ready, 1, square)

            def pre_norm(self, T, n):
                self.stats(T, 0, sq_ready, 1, square)

            def ple(self, l):
                for k in range(KT):
                    self.x_from_norm(k)
                for n in range(4):
                    w = self.unit().rearrange("p (k m) -> p k m", k=KT)
                    for d in range(2):
                        for k in range(KT):
                            m = self.mm(ps[:, n, d * S:d * S + S], w[:, k, d * P:d * P + P], x[:, k, 0:S], k == 0, k == KT - 1)
                    self.done(m)
                w = self.unit().rearrange("p (k m) -> p k m", k=2)
                for d in range(KT):
                    for k in range(2):
                        m = self.mm(y_tile(S, d), w[:, k, d * P:d * P + P], ple_p[:, l, k, :], k == 0, k == 1)
                self.done(m)

            def mixer(self, l):
                pe, seen = self.pe, self.seen
                for k in range(KT):
                    self.x_from_norm(k)
                pr0 = seen.now(proj_ready)
                for n in range(9):
                    if n >= 4:
                        pe.wait_ge(proj_ready, pr0 + n - 3)
                    w = self.unit().rearrange("p (k m) -> p k m", k=KT)
                    for d in range(2):
                        forget_tile = n == 1 and d == 1
                        M = 8 if forget_tile else P
                        for k in range(KT):
                            m = self.mm(ps[0:M, n % 4, d * S:d * S + S], w[:, k, d * P:d * P + M], x[:, k, 0:S], k == 0, k == KT - 1)
                    if n == 1:
                        for r in range(ST):
                            for k in range(KT):
                                m = self.mm(ps[:, 7, 12 * r:12 * r + 12], x[:, k, r * P:r * P + P],
                                            w[:, k, P + 32:P + 44], k == 0, k == KT - 1)
                    self.done(m)
                for n in range(3):
                    pe.wait_ge(proj_ready, pr0 + 9 + n - 3)
                    self.values(n, (9 + n) % 4, 256)
                seen(proj_ready, 9)
                pe.wait_ge(proj_ready, seen.now(proj_ready))
                pe.wait_ge(gates_ready, seen(gates_ready))
                for bank, (t, swap) in zip((4, 5, 6, 7), ((T_KSLC, "swap64"), (T_NQ, "swap64"), (T_DQ, "swap32"), (T_DK, "swap32"))):
                    self.mm(ps[:, bank, :], c(swap), proj[:, t:t + 2, :], True, True).then_inc(swapped, 1)
                pe.wait_ge(blocks_ready, seen(blocks_ready, 2))
                for n in range(4):
                    w = self.unit().rearrange("p (l m) -> p l m", l=8)
                    for i in range(8):
                        for h in range(2):
                            m = self.mm(ps[:, 0, 2 * NC * h:2 * NC * h + 2 * NC], w[:, i, h * P:h * P + P], block_kv[:, 8 * n + i, :],
                                        n == 0 and i == 0 and h == 0, n == 3 and i == 7, skip_group_check=True)
                    self.done(m)
                pe.wait_ge(val_ready, seen(val_ready, 3))
                w = self.unit()
                for r in range(ST):
                    for k in range(KT):
                        self.mm(ps[:, 1, 256 * r:256 * r + P], x[:, k, r * P:r * P + P], w[:, k * P:k * P + P], k == 0, k == KT - 1)
                two = w[:, KT * P:KT * P + 384]
                wk, wv = two[:, 0:256].rearrange("p (h m) -> p h m", h=2), two[:, 256:384].rearrange("p (h m) -> p h m", h=2)
                pe.wait_ge(gelu_ready, seen(gelu_ready))
                for h in range(2):
                    self.mm(ps[:, 2, 0:NC], wk[:, h, :], hid[:, h, 0:NC], h == 0, h == 1)
                pe.wait_ge(hid4_ready, seen(hid4_ready))
                for h in range(2):
                    m = self.mm(ps[:, 3, 0:64], hid4[:, h, :, :].rearrange("p a b -> p (a b)"), wv[:, h, :], h == 0, h == 1)
                self.done(m)
                pe.wait_ge(kc_raw, seen(kc_raw))
                self.mm(ps[:, 4, 0:NC], c("swap64"), kc[:], True, True).then_inc(kc_swapped, 1)
                pe.wait_ge(rope_ready, seen(rope_ready, 4))
                pe.wait_ge(kc_ready, seen(kc_ready, 2))
                pe.wait_ge(val_ready, seen(val_ready, 1))
                for t in range(ST):
                    for h in (0, 2, 1, 3):
                        q = slice(64 * (h % 2), 64 * (h % 2) + 64)
                        at = (2 * t + h // 2) * 16
                        m = self.mm(ps[:, 5 + h % 2, at:at + NC], proj[q, T_NQ + h // 2, t * P:t * P + P], kc[q, :], True, True)
                m.then_inc(cmp_scores, 1)
                pe.wait_ge(cmp_probs, seen(cmp_probs))
                for t in range(ST):
                    m = nc.tensor.transpose(ps[:, 7, t * P:t * P + P], sc[:, t, :, :].rearrange("p a b -> p (a b)"), c("ident"))
                m.then_inc(cmp_turned, 1)
                pe.wait_ge(cmp_t, seen(cmp_t))
                for t in range(ST):
                    m = self.mm(ps[:, 7, t * 256:t * 256 + 256], pc_t[:, t, :], vc_diag[:], True, True)
                m.then_inc(cmp_out, 1)
                pe.wait_ge(forget_ready, seen(forget_ready))

                def scores(j, bank):
                    t, maps, _, _ = JOBS[j]
                    kw = (t + 1) * P
                    for m, (qt, kt, p0, wd, _, fh) in enumerate(maps):
                        rows = slice(p0, p0 + wd)
                        at = m * S
                        self.mm(ps[:, bank, at:at + kw], proj[rows, qt, t * P:t * P + P], proj[rows, kt, 0:kw],
                                True, False, skip_group_check=True)
                        if fh is not None:
                            self.mm(ps[:, bank, at:at + kw], c("ident", slice(0, 8))[:, fh:fh + 1].broadcast_to([8, P]), forget[:, 0:kw],
                                    False, False, skip_group_check=True)
                        o = self.mm(ps[:, bank, at + t * P:at + kw], c("ident"), c("low"), False, True, skip_group_check=True)
                    o.then_inc(score_ready, 1)

                def blocks(j):
                    t, maps, _, _ = JOBS[j]
                    return [(m, kb, m * S + kb * P, V) for m, (_, _, _, _, V, _) in enumerate(maps) for kb in range(t + 1)]

                self.jobs(len(JOBS), 2, scores, blocks, lambda j, kb, V: val[:, kb, V:V + 64], lambda j: JOBS[j][0] + 1)
                self.turn_heads()
                self.project_out(S)

            def values(self, n, bank, N):
                w = self.unit().rearrange("p (k m) -> p k m", k=KT)
                for r in range(ST):
                    for k in range(KT):
                        m = self.mm(ps[:, bank, 256 * r:256 * r + N], x[:, k, r * P:r * P + P], w[:, k, 0:N], k == 0, k == KT - 1)
                self.done(m)

            def jobs(self, n, maps, scores, blocks, v_of, kbs):
                pe, seen = self.pe, self.seen
                e0, p0, o0 = seen.now(exp_done), seen.now(probs_t_ready), seen.now(out_taken)
                for j in range(n + 2):
                    if j < n:
                        if j >= 3:
                            pe.wait_ge(exp_done, e0 + maps * (j - 2))
                        scores(j, j % 3)
                    if 1 <= j <= n:
                        a = j - 1
                        pe.wait_ge(exp_done, e0 + maps * (a + 1))
                        if a >= 2:
                            pe.wait_ge(probs_t_ready, p0 + a - 1)
                        for i, (m, kb, at, V) in enumerate(blocks(a)):
                            o = nc.tensor.transpose(ps[:, 3 + a % 2, i * P:i * P + P], probs[:, a % 3, at:at + P], c("ident"))
                        o.then_inc(turned, 1)
                    if j >= 2:
                        a = j - 2
                        pe.wait_ge(probs_t_ready, p0 + a + 1)
                        if a >= 2:
                            pe.wait_ge(out_taken, o0 + a - 1)
                        for i, (m, kb, at, V) in enumerate(blocks(a)):
                            o = self.mm(ps[:, 5 + a % 2, m * 64:m * 64 + 64], probs_t[:, a % 2, i * P:i * P + P], v_of(a, kb, V),
                                        kb == 0, kb == kbs(a) - 1)
                        o.then_inc(out_ready, 1)
                seen(exp_done, maps * n), seen(probs_t_ready, n), seen(out_taken, n)

            def turn_heads(self):
                pe, seen = self.pe, self.seen
                pe.wait_ge(rms_act, seen(rms_act))
                for t in range(ST):
                    for b in range(2):
                        for i in range(4):
                            o = nc.tensor.transpose(ps[:, 2 * t + b, i * P:i * P + P], heads[:, t, (4 * b + i) * P:(4 * b + i) * P + P], c("ident"))
                        o.then_inc(heads_turned, 1)

            def project_out(self, T):
                self.pe.wait_ge(heads_ready, self.seen(heads_ready, 4))
                self.square_product(T)

            def square_product(self, T):
                for n in range(4):
                    w = self.unit().rearrange("p (k m) -> p k m", k=KT)
                    for d in range(2):
                        for k in range(KT):
                            m = self.mm(y_tile(T, 2 * n + d), w[:, k, d * P:d * P + P], z[:, k, 0:T], k == 0, k == KT - 1)
                    self.done(m)

            def ada(self, l):
                if l == 0:
                    self.pe.wait_ge(cs_ready, 1)
                self.pe.wait_ge(res_ready, self.seen(res_ready, 4 if l == 0 else 0))
                for n in range(36):
                    w = self.unit().rearrange("p (k m) -> p k m", k=KT)
                    for d in range(2):
                        for k in range(KT):
                            at = 2 * (2 * n + d)
                            m = self.mm(ps[:, 7, at:at + 2], w[:, k, d * P:d * P + P], cs[:, k, :], k == 0, k == KT - 1)
                    self.done(m)

            def residual(self, T, g):
                self.seen(res_ready, KT * T // S)

            def conv(self):
                pe, seen = self.pe, self.seen
                for k in range(KT):
                    self.x_from_norm(k, 2)
                c0 = seen.now(conv_ready)
                for n in range(KT):
                    w = self.unit().rearrange("p (g k m) -> p g k m", g=2, k=KT)
                    if n >= 2:
                        pe.wait_ge(gate_sum, seen.now(gate_sum) + n - 1)
                    for g in range(2):
                        for k in range(KT):
                            m = self.mm(ps[:, 2 * (n % 2) + g, :], w[:, g, k, :], z[:, k, :], k == 0, k == KT - 1)
                    self.done(m)
                seen(gate_sum, KT)
                self.stats(512, 0, z_ready, 1, square2)
                self.stats(512, 1, sq_ready, 1, square3)
                for k in range(KT):
                    self.x_from_norm(k, 1)
                self.square_product(512)

            def attention(self):
                pe, seen = self.pe, self.seen
                for k in range(KT):
                    self.x_from_norm(k, 2)
                pr0 = seen.now(proj_ready)
                for n in range(5):
                    w = self.unit().rearrange("p (k m) -> p k m", k=KT)
                    if n == 4:
                        pe.wait_ge(proj_ready, pr0 + 1)
                    for d in range(2):
                        for k in range(KT):
                            o = ps[:, n % 4, d * S:d * S + S] if n < 4 else ps[:, 4 + d, :]
                            m = self.mm(o, w[:, k, d * P:d * P + P], z[:, k, 0:S if n < 4 else 512], k == 0, k == KT - 1)
                    self.done(m)
                w = self.unit().rearrange("p (k m) -> p k m", k=KT)
                for r in range(4):
                    for k in range(KT):
                        m = self.mm(ps[:, 6 + r // 2, 256 * (r % 2):256 * (r % 2) + 256], z[:, k, r * P:r * P + P], w[:, k, :], k == 0, k == KT - 1)
                self.done(m)
                pe.wait_ge(proj_ready, seen(proj_ready, 6))
                for n in range(4):
                    self.mm(ps[:, n, :], c("swapax"), q_at[:, 2 * n:2 * n + 2, :], True, True).then_inc(swapped, 1)
                self.mm(ps[:, 4, :], c("swapax"), k_at[:, :, 0:S], True, True).then_inc(swapped, 1)
                pe.wait_ge(val_ready, seen(val_ready, 1))
                pe.wait_ge(rope_ready, seen(rope_ready, 5))

                def scores(j, bank):
                    t, p, g, i = JOBS2[j]
                    rows = slice(64 * i, 64 * i + 64)
                    self.mm(ps[:, bank, :], q_at[rows, 4 * p + g, t * P:t * P + P], k_at[rows, p, :], True, False, skip_group_check=True)
                    o = self.mm(ps[:, bank, P:2 * P] if t == 0 else ps[:, bank, 0:P], c("ident"), c("low" if t == 0 else "high"),
                                False, True, skip_group_check=True)
                    o.then_inc(score_ready, 1)

                def v_of(j, kb, V):
                    t, p, g, i = JOBS2[j]
                    return v_at[:, kb, 64 * (2 * p + i):64 * (2 * p + i) + 64]

                self.jobs(len(JOBS2), 1, scores, lambda j: [(0, kb, kb * P, None) for kb in range(4)], v_of, lambda j: 4)
                self.turn_heads()
                self.project_out(S)

            def finish(self):
                self.stats(S, 0, sq_ready, 1, square)

        square2 = z
        square3 = hidden

        @block.tensor
        def _(pe):
            stages(PE(pe))

        class Act(Engine):
            def __init__(self, act):
                self.act, self.seen, self.u = act, Seen(), 0
                self.x_from_prev = self.x_from_norm = None

            def f(self, out, in_, func, **kw):
                return nc.scalar.activation(out, in_, func, **kw)

            def start(self):
                self.hid_base = RING
                self.act.wait_ge(params_landed, 64)
                self.f(cs[:].rearrange("p k c -> p (k c)"), c("csil"), ACT.Silu).then_inc(cs_ready, 1)

            def unit(self, n=1):
                self.u += n
                self.act.wait_ge(unit_done, self.u)

            def ffn(self, T, xin, x_from, x_per):
                act, u0, h0 = self.act, self.u, self.hid_base
                with act.Fori(0, LOOPS) as i:
                    for j in range(RING):
                        act.wait_ge(unit_done, i * RING + (u0 + j + 1))
                        prev = j - 2 if j >= 2 else (RING - 1 if j == 0 else RING - 2) - RING
                        act.wait_ge(hidden_ready, i * RING + (h0 + prev + 1))
                        g = ps[:, 2 * (j % 2), :] if T == 512 else ps[:, j % 4, 0:S]
                        self.f(gated[:, j % 2, 0:T], g, ACT.Silu).then_inc(silu_ready, 1)
                self.u += FT + FT // 2
                self.hid_base += FT

            def post_norm(self, scale, eps, g, b):
                act, seen = self.act, self.seen
                for k in range(0, KT, 2):
                    act.wait_ge(dev_ready, seen(dev_ready))
                    self.f(square[:, k:k + 2, 0:S], z[:, k:k + 2, 0:S], ACT.Square).then_inc(sq_ready, 1)
                act.wait_ge(stat_ready, seen(stat_ready, 2))
                self.f(std[:, 0:S], ps[:, 1, 0:S], ACT.Sqrt, bias=c("eps")[:, eps:eps + 1]).then_inc(std_ready, 1)
                for k in range(KT):
                    act.wait_ge(scaled_ready, seen(scaled_ready))
                    self.f(x[:, k, 0:S], x[:, k, 0:S], ACT.Identity, bias=b[:, k:k + 1]).then_inc(norm_ready, 1)

            def pre_norm(self, T, n):
                act, seen = self.act, self.seen
                for k in range(0, KT, 2):
                    act.wait_ge(res_ready, seen(res_ready, self.res_per))
                    self.f(square[:, k:k + 2, 0:T], x[:, k:k + 2, 0:T], ACT.Square).then_inc(sq_ready, 1)
                act.wait_ge(stat_ready, seen(stat_ready))
                self.f(std[:, 0:T], ps[:, 0, 0:T], ACT.Sqrt, bias=c("eps")[:, 2:3]).then_inc(std_ready, 1)
                act.wait_ge(mods_ready, seen(mods_ready, 1 if n == 0 else 0))
                for k in range(KT):
                    for h, cols in enumerate(halves(T)):
                        act.wait_ge(scaled_ready, seen(scaled_ready))
                        self.f(z[:, k, cols], z[:, k, cols], ACT.Identity, bias=mods[:, 3 * n, k, h:h + 1]).then_inc(norm_ready, 1)

            def ple(self, l):
                for n in range(4):
                    self.unit()
                    for d in range(2):
                        k = 2 * n + d
                        self.f(z[:, k, 0:S], ps[:, n, d * S:d * S + S], ACT.Sigmoid,
                               bias=c(f"ple_b{l}")[:, k:k + 1]).then_inc(sig_ready, 1)
                self.u += 1
                self.res_per = 1
                if l == 0:
                    self.seen(res_ready, 4)

            def mixer(self, l):
                act, seen = self.act, self.seen
                for n in range(9):
                    self.unit()
                    if n == 1:
                        self.f(proj[:, 2, :], ps[:, 1, 0:S], ACT.Copy)
                        self.f(proj[0:8, 3, :], ps[0:8, 1, S:512], ACT.Copy).then_inc(proj_ready, 1)
                        self.f(gates[:], ps[:, 7, 0:24], ACT.Sigmoid).then_inc(gates_ready, 1)
                    else:
                        self.f(proj[:, 2 * n:2 * n + 2, :], ps[:, n % 4, :], ACT.Copy, scale=PROJ_SCALE[n]).then_inc(proj_ready, 1)
                act.wait_ge(forget_in, seen(forget_in))
                self.f(fl[:, 0, :], fl[:, 3, :], ACT.Abs).then_inc(act_step, 1)
                act.wait_ge(act_step, seen(act_step))
                self.f(fl[:, 1, :], fl[:, 0, :], ACT.Exp, scale=-1.0).then_inc(act_step, 1)
                act.wait_ge(act_step, seen(act_step))
                self.f(fl[:, 1, :], fl[:, 1, :], ACT.Ln, bias=c("eps", slice(0, 8))[:, 3:4]).then_inc(forget_act, 1)
                act.wait_ge(lam_in, seen(lam_in))
                self.f(lam_s[:, 0:2], lam_s[:, 0:2], ACT.Exp).then_inc(lam_act, 1)
                self.u += 3
                self.unit(4)
                self.f(hid[:].rearrange("p a b -> p (a b)"), ps[:, 0, 0:4 * NC], ACT.Gelu_apprx_tanh).then_inc(gelu_ready, 1)
                self.unit()
                self.f(kc[:], ps[:, 2, 0:NC], ACT.Copy).then_inc(kc_raw, 1)
                act.wait_ge(cmp_in, seen(cmp_in))
                self.f(sc[:].rearrange("p t h c -> p (t h) c")[:, :, 0:NC], sc[:].rearrange("p t h c -> p (t h) c")[:, :, 0:NC],
                       ACT.Exp).then_inc(cmp_exp, 1)
                act.wait_ge(cmp_turned, seen(cmp_turned))
                self.f(pc_t[:].rearrange("p t q -> p (t q)"), ps[:, 7, 0:S], ACT.Copy).then_inc(cmp_t, 1)

                def exps(j, b):
                    t, maps, _, _ = JOBS[j]
                    for m in range(2):
                        self.f(probs[:, b, m * S:m * S + (t + 1) * P], ps[:, b, m * S:m * S + (t + 1) * P], ACT.Exp,
                               bias=neg_max[:, j, m:m + 1], accum_out=sums[:, j, m:m + 1]).then_inc(exp_done, 1)

                self.jobs(len(JOBS), exps)
                act.wait_ge(rms_in, seen(rms_in))
                self.f(rms[:], rms[:], ACT.Sqrt, bias=c("eps")[:, 1:2], scale=1.0 / 64).then_inc(forget_act, 1)
                self.turn_heads()
                self.u += 4

            def jobs(self, n, exps):
                act, seen = self.act, self.seen
                m0, t0 = seen.now(max_ready), seen.now(turned)
                for j in range(n):
                    act.wait_ge(max_ready, m0 + j + 1)
                    if j >= 3:
                        act.wait_ge(turned, t0 + j - 2)
                    exps(j, j % 3)
                seen(max_ready, n), seen(turned, n)

            def turn_heads(self):
                act, seen = self.act, self.seen
                for t in range(ST):
                    for b in range(2):
                        act.wait_ge(heads_turned, seen(heads_turned))
                        self.f(z[:, 4 * b:4 * b + 4, t * P:t * P + P], ps[:, 2 * t + b, :].rearrange("p (k q) -> p k q", k=4),
                               ACT.Copy).then_inc(heads_ready, 1)

            def ada(self, l):
                self.u += 36

            def residual(self, T, g):
                self.res_per = 2 * T // S

            def conv(self):
                act, seen = self.act, self.seen
                for n in range(KT):
                    self.unit()
                    if n >= 2:
                        act.wait_ge(gate_sum, seen.now(gate_sum) + n - 1)
                    self.f(gated[:, n % 2, :], ps[:, 2 * (n % 2) + 1, :], ACT.Sigmoid,
                           bias=c("pw1_b")[:, KT + n:KT + n + 1]).then_inc(sig_ready, 1)
                seen(gate_sum, KT)
                for k in range(0, KT, 2):
                    act.wait_ge(dev_ready, seen(dev_ready))
                    self.f(square3[:, k:k + 2, :], z[:, k:k + 2, :], ACT.Square).then_inc(sq_ready, 1)
                act.wait_ge(stat_ready, seen(stat_ready, 2))
                self.f(std[:], ps[:, 1, :], ACT.Sqrt, bias=c("eps")[:, 2:3]).then_inc(std_ready, 1)
                for k in range(KT):
                    act.wait_ge(scaled_ready, seen(scaled_ready))
                    self.f(z[:, k, :], z[:, k, :], ACT.Silu, bias=c("conv_ln_b")[:, k:k + 1]).then_inc(norm_ready, 1)
                self.u += 4

            def attention(self):
                act, seen = self.act, self.seen
                for n in range(5):
                    self.unit()
                    if n < 4:
                        self.f(q_at[:, 2 * n:2 * n + 2, :], ps[:, n, :], ACT.Copy, scale=64 ** -0.5).then_inc(proj_ready, 1)
                    else:
                        for d in range(2):
                            self.f(k_at[:, d, :], ps[:, 4 + d, :], ACT.Copy).then_inc(proj_ready, 1)
                self.unit()
                for i in range(2):
                    ins = self.f(v_at[:, 2 * i:2 * i + 2, :], ps[:, 6 + i, :], ACT.Copy)
                ins.then_inc(val_ready, 1)

                def exps(j, b):
                    self.f(probs[:, b, :], ps[:, b, :], ACT.Exp, bias=neg_max[:, j, 0:1], accum_out=sums[:, j, 0:1]).then_inc(exp_done, 1)
                    t, p, g, i = JOBS2[j]
                    h = 4 * (2 * p + i) + g
                    self.f(sink_e[:, j:j + 1], c("sink")[:, h:h + 1], ACT.Exp, bias=neg_max[:, j, 0:1]).then_inc(kc_sum, 1)

                self.jobs(len(JOBS2), exps)
                self.turn_heads()
                self.u += 4

            def finish(self):
                act, seen = self.act, self.seen
                for k in range(0, KT, 2):
                    act.wait_ge(res_ready, seen(res_ready, self.res_per))
                    self.f(square[:, k:k + 2, 0:S], x[:, k:k + 2, 0:S], ACT.Square).then_inc(sq_ready, 1)
                act.wait_ge(stat_ready, seen(stat_ready))
                self.f(std[:, 0:S], ps[:, 0, 0:S], ACT.Sqrt, bias=c("eps")[:, 2:3]).then_inc(std_ready, 1)

        @block.scalar
        def _(act):
            stages(Act(act))

        class Dve(Engine):
            def __init__(self, dve):
                self.dve, self.seen, self.u, self.steps = dve, Seen(), 0, 0
                self.x_from_prev = self.x_from_norm = None

            def start(self):
                v = self.dve
                self.hid_base = RING
                nc.vector.memset(gated[:, :, :], 0.0).then_inc(hidden_ready, RING)
                for buf in (block_kv, hid4, vc_diag, sc):
                    self.link(nc.vector.memset(buf[:], 0.0))
                v.wait_ge(params_landed, 64)

            def link(self, ins):
                self.steps += 1
                ins.then_inc(dve_step, 1)
                self.dve.wait_ge(dve_step, self.steps)

            def unit(self, n=1):
                self.u += n
                self.dve.wait_ge(unit_done, self.u)

            def tt(self, out, a, b, op):
                return nc.vector.tensor_tensor(out, a, b, op)

            def stt(self, out, a, s, b, op0, op1):
                return nc.vector.scalar_tensor_tensor(out, a, s, b, op0, op1)

            def ts(self, out, a, s1, s2, op0, op1=None):
                return nc.vector.tensor_scalar(out, a, s1, s2, op0, op1) if op1 is not None else nc.vector.tensor_scalar(out, a, s1, None, op0)

            def ffn(self, T, xin, x_from, x_per):
                v, seen = self.dve, self.seen
                s0 = seen.now(silu_ready)
                h = hidden[:].rearrange("p (i j) n -> p i j n", i=LOOPS)
                with v.Fori(0, LOOPS) as i:
                    for j in range(RING):
                        v.wait_ge(silu_ready, i * RING + (s0 + j + 1))
                        up = ps[:, 2 * (j % 2) + 1, :] if T == 512 else ps[:, j % 4, S:512]
                        self.tt(h[:, i, j, 0:T], gated[:, j % 2, 0:T], up, ALU.mult).then_inc(hidden_ready, 1)
                seen(silu_ready, FT)
                self.hid_base += FT
                self.u += FT
                self.unit(FT // 2)

            def post_norm(self, scale, eps, g, b):
                v, seen = self.dve, self.seen
                for n in range(4):
                    self.stt(z[:, 2 * n:2 * n + 2, 0:S], x[:, 2 * n:2 * n + 2, 0:S], scale, y_bank(n), ALU.mult, ALU.add).then_inc(z_ready, 1)
                v.wait_ge(z_ready, seen(z_ready, 4))
                v.wait_ge(stat_ready, seen(stat_ready))
                for n in range(4):
                    self.tt(z[:, 2 * n:2 * n + 2, 0:S], z[:, 2 * n:2 * n + 2, 0:S],
                            ps[:, 0, 0:S].unsqueeze(1).broadcast_to([P, 2, S]), ALU.subtract).then_inc(dev_ready, 1)
                v.wait_ge(dev_ready, seen(dev_ready, 4))
                seen(stat_ready)
                v.wait_ge(std_ready, seen(std_ready))
                self.link(nc.vector.reciprocal(rstd[:, 0:S], std[:, 0:S]))
                for k in range(KT):
                    self.stt(x[:, k, 0:S], z[:, k, 0:S], g[:, k:k + 1], rstd[:, 0:S], ALU.mult, ALU.mult).then_inc(scaled_ready, 1)
                v.wait_ge(norm_ready, seen(norm_ready, KT))

            def pre_norm(self, T, n):
                v, seen = self.dve, self.seen
                v.wait_ge(std_ready, seen(std_ready))
                seen(stat_ready)
                self.link(nc.vector.reciprocal(rstd[:, 0:T], std[:, 0:T]))
                for k in range(KT):
                    for h, cols in enumerate(halves(T)):
                        self.stt(z[:, k, cols], x[:, k, cols], mod_a[:, n, k, h:h + 1], rstd[:, cols], ALU.mult, ALU.mult).then_inc(scaled_ready, 1)
                seen(norm_ready, KT * T // S)

            def ple(self, l):
                v, seen = self.dve, self.seen
                self.unit(5)
                for n in range(4):
                    v.wait_ge(sig_ready, seen(sig_ready, 2))
                    self.link(self.tt(z[:, 2 * n:2 * n + 2, 0:S], z[:, 2 * n:2 * n + 2, 0:S], y_bank(n), ALU.mult))
                    self.tt(x[:, 2 * n:2 * n + 2, 0:S], x[:, 2 * n:2 * n + 2, 0:S], z[:, 2 * n:2 * n + 2, 0:S], ALU.add).then_inc(res_ready, 1)
                v.wait_ge(res_ready, seen(res_ready, 4))

            def rotate(self, x2, bank, name, w=None):
                cos, sin = (c(f"{name}_{n}").unsqueeze(1).broadcast_to([P, 2, S]) for n in ("cos", "sin"))
                v, seen = self.dve, self.seen
                v.wait_ge(swapped, seen(swapped))
                t = tmp[:, 0, :].rearrange("p (a s) -> p a s", a=2)
                self.tt(t, ps[:, bank, :].rearrange("p (a s) -> p a s", a=2), sin, ALU.mult)
                self.link(self.tt(x2, x2, cos, ALU.mult))
                self.tt(x2, x2, t, ALU.add).then_inc(rope_ready, 1)
                v.wait_ge(rope_ready, seen(rope_ready))

            def mixer(self, l):
                v, seen = self.dve, self.seen
                lam_init = 0.8 - 0.6 * math.exp(-0.3 * l)
                lp = c(f"lam{l}").rearrange("p (a b) -> p a b", a=4)
                self.link(self.tt(lam_t[:].rearrange("p (a b) -> p a b", a=2), lp[:, 0:4:2, :], lp[:, 1:4:2, :], ALU.mult))
                nc.vector.tensor_reduce(lam_s[:, 0:2], lam_t[:].rearrange("p (a b) -> p a b", a=2), AX.X, ALU.add).then_inc(lam_in, 1)
                self.ts(subg[:], c(f"subln{l}"), 1.0 - lam_init, None, ALU.mult)
                v.wait_ge(proj_ready, seen(proj_ready, 2))
                self.link(self.ts(fl[:, 3, :], proj[0:8, T_FORGET, :], c(f"fox_b{l}", slice(0, 8)), None, ALU.add))
                self.ts(fl[:, 2, :], fl[:, 3, :], 0.0, None, ALU.min).then_inc(forget_in, 1)
                raw = proj[:, T_CMP, :]
                for half in range(2):
                    rows = slice(64 * half, 64 * half + 64)
                    a = raw[rows, :]
                    window = bass.AP(a.tensor, a.offset, [list(a.ap[0]), [1, CMP_BLOCK], [CMP_STRIDE, NC]])
                    pos = c(f"pos{l}", rows).unsqueeze(2).broadcast_to([64, CMP_BLOCK, NC])
                    self.tt(block_kv[rows, :, NC * half:NC * half + NC], window, pos, ALU.add).then_inc(blocks_ready, 1)
                self.u += 9
                for n in range(3):
                    self.unit()
                    nc.vector.tensor_copy(val[:, :, 256 * n:256 * n + 256], ps[:, (9 + n) % 4, :].rearrange("p (r m) -> p r m", r=2)).then_inc(val_ready, 1)
                v.wait_ge(proj_ready, seen(proj_ready, 7))
                self.rotate(proj[:, T_KSLC:T_KSLC + 2, :], 4, "nsa")
                self.rotate(proj[:, T_NQ:T_NQ + 2, :], 5, "nsa")
                self.rotate(proj[:, T_DQ:T_DQ + 2, :], 6, "diff")
                self.rotate(proj[:, T_DK:T_DK + 2, :], 7, "diff")
                v.wait_ge(forget_act, seen(forget_act))
                self.link(self.tt(fl[:, 3, :], fl[:, 1, :], fl[:, 2, :], ALU.subtract))
                nc.vector.tensor_tensor_scan(forget[:], fl[:, 3, :], fl[:, 3, :], 0.0, ALU.add, ALU.bypass).then_inc(forget_ready, 1)
                v.wait_ge(lam_act, seen(lam_act))
                self.link(self.stt(lam_s[:, 2:3], lam_s[:, 1:2], -lam_init, lam_s[:, 0:1], ALU.add, ALU.subtract))
                v.wait_ge(gelu_ready, seen(gelu_ready))
                self.u += 4
                nc.vector.tensor_copy(hid4[:, :, :, 0:NC], hid[:, :, NC:2 * NC].unsqueeze(2).broadcast_to([P, 2, 4, NC])).then_inc(hid4_ready, 1)
                self.unit()
                nc.vector.tensor_copy(val[:, :, 768:896], ps[:, 1, :].rearrange("p (r m) -> p r m", r=2)[:, :, 0:P]).then_inc(val_ready, 1)
                for h in range(4):
                    i = nc.vector.tensor_copy(vc_diag[32 * h:32 * h + 32, 64 * h:64 * h + 64], ps[32 * h:32 * h + 32, 3, 0:64])
                i.then_inc(kc_ready, 1)
                v.wait_ge(kc_swapped, seen(kc_swapped))
                self.link(self.tt(kc_t[:], ps[:, 4, 0:NC], c("kc_sin"), ALU.mult))
                self.link(self.tt(kc[:], kc[:], c("kc_cos"), ALU.mult))
                self.tt(kc[:], kc[:], kc_t[:], ALU.add).then_inc(kc_ready, 1)
                v.wait_ge(cmp_scores, seen(cmp_scores))
                add = c("cmp_add").rearrange("p (t c) -> p t c", t=ST).unsqueeze(2).broadcast_to([P, ST, 2, NC])
                for i in range(2):
                    src = ps[:, 5 + i, 0:64].rearrange("p (t s c) -> p t s c", t=ST, s=2)[:, :, :, 0:NC]
                    self.link(self.tt(sc[:, :, i:4:2, 0:NC], src, add, ALU.add))
                s3 = sc[:].rearrange("p t h c -> p (t h) c")[:, :, 0:NC]
                self.link(nc.vector.tensor_reduce(cmp_m[:], s3, AX.X, ALU.max))
                self.tt(s3, s3, cmp_m[:].unsqueeze(2).broadcast_to([P, 8, NC]), ALU.subtract).then_inc(cmp_in, 1)
                v.wait_ge(cmp_exp, seen(cmp_exp))
                self.link(nc.vector.tensor_reduce(cmp_s[:], s3, AX.X, ALU.add))
                self.link(nc.vector.reciprocal(cmp_m[:], cmp_s[:]))
                for t in range(ST):
                    mul = c("cmp_mul")[:, t * NC:t * NC + NC].unsqueeze(1).broadcast_to([P, 4, NC])
                    i = self.tt(sc[:, t, :, 0:NC], sc[:, t, :, 0:NC], mul, ALU.mult)
                i.then_inc(cmp_probs, 1)
                g = gates[:].rearrange("p t (h b) -> p t h b", h=4)
                self.link(self.tt(cmp_s[:].rearrange("p (t h) -> p t h", t=ST), cmp_m[:].rearrange("p (t h) -> p t h", t=ST), g[:, :, :, 0], ALU.mult))
                v.wait_ge(cmp_out, seen(cmp_out))
                for t in range(ST):
                    i = self.tt(heads[:, t, 0:256].rearrange("p (h d) -> p h d", h=4), ps[:, 7, t * 256:t * 256 + 256].rearrange("p (h d) -> p h d", h=4),
                                cmp_s[:, 4 * t:4 * t + 4].unsqueeze(2).broadcast_to([P, 4, 64]), ALU.mult)
                self.link(i)

                def maxima(j, b):
                    t = JOBS[j][0]
                    nc.vector.tensor_reduce(neg_max[:, j, :], ps[:, b, :].rearrange("p (m k) -> p m k", m=2)[:, :, 0:(t + 1) * P],
                                            AX.X, ALU.max, negate=True).then_inc(max_ready, 1)

                def take(j, b):
                    t, maps, kind, at = JOBS[j]
                    self.link(nc.vector.reciprocal(coef[:, j, :], sums[:, j, :]))
                    if kind in ("slc", "win"):
                        h = at // 64
                        self.link(self.tt(coef[:, j, :], coef[:, j, :], g[:, t, h:4:2, 1 if kind == "slc" else 2], ALU.mult))
                    if kind == "diff1":
                        self.link(self.ts(coef[:, j, :], coef[:, j, :], lam_s[:, 2:3], None, ALU.mult))
                    dst = heads[:, t, at:at + 256].rearrange("p (m d) -> p m d", m=2)[:, :, 0:64] if at + 256 <= D else \
                        bass.AP(heads.tensor, heads[:, t, at:at + 64].offset, [list(heads.ap[0]), [P, 2], [1, 64]])
                    src = ps[:, 5 + b, 0:P].rearrange("p (m d) -> p m d", m=2)
                    cf = coef[:, j, :].unsqueeze(2).broadcast_to([P, 2, 64])
                    v.wait_ge(out_ready, seen(out_ready))
                    if kind in ("fox", "diff0"):
                        self.tt(dst, src, cf, ALU.mult).then_inc(out_taken, 1)
                    else:
                        half = tmp[:, 0, 0:P].rearrange("p (m d) -> p m d", m=2)
                        self.tt(half, src, cf, ALU.mult).then_inc(out_taken, 1)
                        v.wait_ge(out_taken, self.taken0 + j + 1)
                        self.link(self.tt(dst, dst, half, ALU.add))

                def copy(j, b):
                    n = 2 * (JOBS[j][0] + 1) * P
                    nc.vector.tensor_copy(probs_t[:, b, 0:n], ps[:, 3 + b, 0:n]).then_inc(probs_t_ready, 1)

                self.jobs(len(JOBS), maxima, copy, take)
                sq = tmp[:].rearrange("p a (h d) -> p a h d", h=8)[:, :, 0:4, :]
                od = heads[:, :, 256:512].rearrange("p t (h d) -> p t h d", h=4)
                for t in range(ST):
                    i = self.tt(sq[:, t], od[:, t], od[:, t], ALU.mult)
                self.link(i)
                nc.vector.tensor_reduce(rms[:].rearrange("p (t h) -> p t h", t=ST), sq, AX.X, ALU.add).then_inc(rms_in, 1)
                v.wait_ge(forget_act, seen(forget_act))
                self.link(nc.vector.reciprocal(rms[:], rms[:]))
                for t in range(ST):
                    self.link(self.tt(od[:, t], od[:, t], rms[:, 4 * t:4 * t + 4].unsqueeze(2).broadcast_to([P, 4, 64]), ALU.mult))
                    i = self.tt(od[:, t], od[:, t], subg[:].unsqueeze(1).broadcast_to([P, 4, 64]), ALU.mult)
                i.then_inc(rms_act, 1)
                seen(heads_turned, 4)
                self.unit(4)

            def jobs(self, n, maxima, copy, take):
                v, seen = self.dve, self.seen
                s0, t0 = seen.now(score_ready), seen.now(turned)
                self.taken0 = seen.now(out_taken)
                for j in range(n + 2):
                    if j < n:
                        v.wait_ge(score_ready, s0 + j + 1)
                        maxima(j, j % 3)
                    if 1 <= j <= n:
                        v.wait_ge(turned, t0 + j)
                        copy(j - 1, (j - 1) % 2)
                    if j >= 2:
                        take(j - 2, (j - 2) % 2)
                v.wait_ge(out_taken, seen(out_taken, n))
                seen(score_ready, n), seen(turned, n)

            def ada(self, l):
                v, seen = self.dve, self.seen
                self.unit(36)
                b = c(f"ada_b{l}").unsqueeze(2).broadcast_to([P, NMOD * KT, 2])
                self.link(self.tt(mods[:].rearrange("p a k c -> p (a k) c"), ps[:, 7, 0:2 * NMOD * KT].rearrange("p (a c) -> p a c", c=2), b, ALU.add))
                for n in range(3):
                    gn = c(f"norm_g{l}")[:, n * KT:n * KT + KT].unsqueeze(2).broadcast_to([P, KT, 2])
                    self.stt(mod_a[:, n], mods[:, 3 * n + 1], 1.0, gn, ALU.add, ALU.mult)
                for n in (2, 8):
                    i = self.ts(mods[:, n], mods[:, n], 0.5, None, ALU.mult)
                i.then_inc(mods_ready, 1)
                v.wait_ge(mods_ready, seen(mods_ready))

            def residual(self, T, g):
                v, seen = self.dve, self.seen
                for k in range(KT):
                    for h, cols in enumerate(halves(T)):
                        self.stt(x[:, k, cols], y_tile(T, k)[:, cols], mods[:, g, k, h:h + 1], x[:, k, cols], ALU.mult, ALU.add).then_inc(res_ready, 1)
                v.wait_ge(res_ready, seen(res_ready, KT * T // S))

            def conv(self):
                v, seen = self.dve, self.seen
                for n in range(KT):
                    nc.vector.memset(conv_in[:, n, :, 0:PAD], 0.0)
                    i = nc.vector.memset(conv_in[:, n, :, PAD + S:], 0.0)
                self.link(i)
                w = c("conv_w").rearrange("p (k t) -> p k t", k=KT)
                for n in range(KT):
                    self.unit()
                    v.wait_ge(sig_ready, seen(sig_ready))
                    self.stt(conv_in[:, n, :, PAD:PAD + S], ps[:, 2 * (n % 2), :].rearrange("p (a s) -> p a s", a=2), c("pw1_b")[:, n:n + 1],
                             gated[:, n % 2, :].rearrange("p (a s) -> p a s", a=2), ALU.add, ALU.mult).then_inc(gate_sum, 1)
                    v.wait_ge(gate_sum, seen(gate_sum))
                    acc = ps[:, 4 + n % 2, :].rearrange("p (a s) -> p a s", a=2)
                    self.link(self.ts(acc, conv_in[:, n, :, 0:S], w[:, n, 0:1], c("conv_b")[:, n:n + 1], ALU.mult, ALU.add))
                    for t in range(1, TAPS):
                        dst = acc if t < TAPS - 1 else cv[:, n, :].rearrange("p (a s) -> p a s", a=2)
                        self.link(self.stt(dst, conv_in[:, n, :, t:t + S], w[:, n, t:t + 1], acc, ALU.mult, ALU.add))
                for k in range(0, KT, 2):
                    nc.vector.tensor_copy(z[:, k:k + 2, :], cv[:, k:k + 2, :]).then_inc(z_ready, 1)
                v.wait_ge(z_ready, seen(z_ready, 4))
                v.wait_ge(stat_ready, seen(stat_ready))
                for k in range(0, KT, 2):
                    self.tt(z[:, k:k + 2, :], z[:, k:k + 2, :], ps[:, 0, :].unsqueeze(1).broadcast_to([P, 2, 512]), ALU.subtract).then_inc(dev_ready, 1)
                v.wait_ge(dev_ready, seen(dev_ready, 4))
                seen(stat_ready)
                v.wait_ge(std_ready, seen(std_ready))
                self.link(nc.vector.reciprocal(rstd[:], std[:]))
                for k in range(KT):
                    self.stt(z[:, k, :], z[:, k, :], c("conv_ln_g")[:, k:k + 1], rstd[:], ALU.mult, ALU.mult).then_inc(scaled_ready, 1)
                for k in range(KT):
                    for h, cols in enumerate(halves(512)):
                        self.link(self.tt(rms[:, 0:1], c("pw2_b")[:, k:k + 1], mods[:, 5, k, h:h + 1], ALU.mult))
                        self.link(self.ts(x[:, k, cols], x[:, k, cols], rms[:, 0:1], None, ALU.add))
                seen(norm_ready, KT)
                self.unit(4)

            def attention(self):
                v, seen = self.dve, self.seen
                v.wait_ge(proj_ready, seen(proj_ready, 6))
                for n in range(4):
                    self.rotate(q_at[:, 2 * n:2 * n + 2, :], n, "ax")
                self.rotate(k_at[:, :, 0:S], 4, "ax")
                self.u += 6

                def maxima(j, b):
                    t, p, g, i = JOBS2[j]
                    h = 4 * (2 * p + i) + g
                    self.link(nc.vector.tensor_reduce(coef[:, j, 0:1], ps[:, b, :], AX.X, ALU.max))
                    self.ts(neg_max[:, j, 0:1], coef[:, j, 0:1], c("sink")[:, h:h + 1], -1.0, ALU.max, ALU.mult).then_inc(max_ready, 1)

                def copy(j, b):
                    nc.vector.tensor_copy(probs_t[:, b, :], ps[:, 3 + b, :]).then_inc(probs_t_ready, 1)

                def take(j, b):
                    t, p, g, i = JOBS2[j]
                    h = 4 * (2 * p + i) + g
                    v.wait_ge(kc_sum, seen(kc_sum))
                    self.link(self.tt(sums[:, j, 0:1], sums[:, j, 0:1], sink_e[:, j:j + 1], ALU.add))
                    self.link(nc.vector.reciprocal(coef[:, j, 1:2], sums[:, j, 0:1]))
                    v.wait_ge(out_ready, seen(out_ready))
                    self.ts(heads[:, t, 64 * h:64 * h + 64], ps[:, 5 + b, 0:64], coef[:, j, 1:2], None, ALU.mult).then_inc(out_taken, 1)

                self.jobs(len(JOBS2), maxima, copy, take)
                self.ts(rms[:, 0:1], coef[:, 0, 0:1], 1.0, None, ALU.mult).then_inc(rms_act, 1)
                self.unit(4)

            def finish(self):
                v, seen = self.dve, self.seen
                v.wait_ge(std_ready, seen(std_ready))
                self.link(nc.vector.reciprocal(rstd[:, 0:S], std[:, 0:S]))
                for k in range(KT):
                    i = self.stt(z[:, k, 0:S], x[:, k, 0:S], c("final_g")[:, k:k + 1], rstd[:, 0:S], ALU.mult, ALU.mult)
                i.then_inc(heads_ready, 20)

        cv = carve(KT * 2 * (S + 2 * PAD), KT, 512)

        @block.vector
        def _(dve):
            stages(Dve(dve))

        @block.gpsimd
        def _(pool):
            pool.wait_ge(heads_ready, 4 * 3 + 20)
            pool.dma_start(out, z[:, :, 0:S]).then_inc(stored, 16)
            pool.wait_ge(stored, 16)


def kernel(**inputs):
    import concourse.bacc as bacc
    from concourse.bass_utils import run_bass_kernel_spmd

    inp = {k: np.asarray(v) for k, v in inputs.items()}
    weights = lay_weights(inp)
    n_units = weights.shape[0]
    consts = lay_constants(inp)
    arrays = {
        "weights": weights,
        "consts": consts,
        "x_in": lay_rows(inp["x"]),
        "ctx_in": lay_rows(inp["ctx_2"]),
        "p_in": np.ascontiguousarray(np.stack([inp["p"][l, 0].T.reshape(2, P, S).transpose(1, 0, 2) for l in range(DEPTH)], 1)),
    }
    nc = bacc.Bacc("TRN2", target_bir_lowering=False, num_devices=1)
    aps = {n: nc.dram_tensor(n, a.shape, F32, kind="ExternalInput").ap() for n, a in arrays.items()}
    out = nc.dram_tensor("out", (P, KT, S), F32, kind="ExternalOutput").ap()
    build(nc, aps["weights"], aps["consts"], aps["x_in"], aps["ctx_in"], aps["p_in"], out, n_units)
    r = run_bass_kernel_spmd(nc, [arrays], core_ids=[0])
    got = r.results[0]["out"]
    return np.ascontiguousarray(got.transpose(1, 0, 2).reshape(D, S).T)[None]
```

```python
import math
from contextlib import ExitStack

import numpy as np

import concourse.bass as bass
from concourse import mybir

P = 128
D = 1024
KT = D // P
S = 256
ST = S // P
DEPTH = 2
FF = 2816
FT = FF // P
Q = 512
RING = 11
STEPS = 11
LOOPS = FT // STEPS
AHEAD = 8
GROUPS = 18
NEG = -1e30
ALPHA = (2.0 * DEPTH) ** 0.25
CMP_BLOCK, CMP_STRIDE = 32, 16
NC = (S - CMP_BLOCK) // CMP_STRIDE + 1
HID = 256
TAPS = 31
PAD = (TAPS - 1) // 2
NMOD = 9
PITCH = 32

F32 = mybir.dt.float32
F32R = mybir.dt.float32r
ALU = mybir.AluOpType
ACT = mybir.ActivationFunctionType
AX = mybir.AxisListType

(T_CMP, T_KSLC, T_KWIN, T_FORGET, T_NQ, T_DQ, T_DK, T_FQ, T_FK) = (0, 1, 2, 3, 4, 6, 8, 10, 14)
PROJ_SCALE = [1.0, 1.0, 64 ** -0.5, 32 ** -0.5, 1.0, 64 ** -0.5, 64 ** -0.5, 1.0, 1.0]
V_SLC, V_WIN, V_DIFF, V_FOX, V_ALL = 0, 64, 128, 384, 896


def columns():
    widths = [("ident", P), ("swap64", P), ("swap32", P), ("swapax", P), ("mean", P), ("low", P), ("high", P),
              ("nsa_cos", S), ("nsa_sin", S), ("diff_cos", S), ("diff_sin", S), ("ax_cos", S), ("ax_sin", S),
              ("cmp_add", ST * NC), ("cmp_mul", ST * NC), ("kc_cos", NC), ("kc_sin", NC),
              ("eps", 4), ("csil", KT * 2), ("final_g", KT), ("sink", 16), ("conv_w", KT * TAPS),
              ("conv_b", KT), ("conv_ln_g", KT), ("conv_ln_b", KT), ("pw1_b", 2 * KT), ("pw2_b", KT)]
    for l in range(DEPTH):
        widths += [(f"ln_g{l}", 3 * KT), (f"ln_b{l}", 3 * KT), (f"ple_b{l}", KT), (f"pos{l}", CMP_BLOCK),
                   (f"fox_b{l}", 1), (f"lam{l}", 4 * 32), (f"subln{l}", 64),
                   (f"ada_b{l}", NMOD * KT), (f"norm_g{l}", 3 * KT)]
    at, place = 0, {}
    for name, w in widths:
        place[name] = (at, w)
        at += w
    return place, at


def lay_constants(inp):
    place, width = columns()
    c = np.zeros((P, width), np.float32)

    def put(name, a, rows=slice(0, P)):
        s, w = place[name]
        c[rows, s:s + w] = a

    p = np.arange(P)
    put("ident", np.eye(P, dtype=np.float32))
    for name, block in (("swap64", 64), ("swap32", 32), ("swapax", 32)):
        m = np.zeros((P, P), np.float32)
        other = (p // block) * block + (p % block + block // 2) % block
        m[other, p] = 1.0
        put(name, m)
    put("mean", 1.0 / D)
    put("low", np.where(p[None, :] <= p[:, None], 0.0, NEG))
    put("high", np.where(p[None, :] >= p[:, None], 0.0, NEG))

    def rope_tables(name, dim, pos):
        inv = (np.float32(10000.0) ** (-np.arange(0, dim, 2, dtype=np.float32) / np.float32(dim))).astype(np.float32)
        ang = pos.astype(np.float32)[None, :] * inv[p % (dim // 2)][:, None]
        sign = np.where(p % dim < dim // 2, -1.0, 1.0)[:, None]
        put(f"{name}_cos", np.cos(ang))
        put(f"{name}_sin", np.sin(ang) * sign)

    rope_tables("nsa", 64, np.arange(S))
    rope_tables("diff", 32, np.arange(S))
    ends = np.arange(NC) * CMP_STRIDE + CMP_BLOCK - 1
    rope_tables("kc", 64, ends)
    inv = (np.float32(10000.0) ** (-np.arange(16, dtype=np.float32) / np.float32(16))).astype(np.float32)
    t = np.arange(S)
    where = np.where((p % 64 < 32)[:, None], (t // 64)[None, :], (t % 64)[None, :]).astype(np.float32)
    ang = where * inv[p % 16][:, None]
    put("ax_cos", np.cos(ang))
    put("ax_sin", np.sin(ang) * np.where(p % 32 < 16, -1.0, 1.0)[:, None])
    seen = (ends[None, None, :] <= np.arange(S).reshape(ST, P).T[:, :, None])
    put("cmp_add", np.where(seen, 0.0, NEG).reshape(P, ST * NC))
    put("cmp_mul", np.where(seen, 1.0, 0.0).reshape(P, ST * NC))
    put("eps", np.array([4e-5, 1e-5, 1e-6, 1.0], np.float32))

    def cols(a):
        return a.reshape(-1, P).T

    put("csil", np.stack([cols(inp["c_2"]), cols(inp["c_ctx_2"])], -1).reshape(P, KT * 2))
    put("final_g", cols(inp["final_g_2"]))
    put("sink", np.broadcast_to(inp["attn_sink_2"].reshape(1, 16), (P, 16)))
    put("conv_w", inp["conv_dw_w_2"][0].reshape(TAPS, KT, P).transpose(2, 1, 0).reshape(P, KT * TAPS))
    put("conv_b", cols(inp["conv_dw_b_2"][0]))
    put("conv_ln_g", cols(inp["conv_ln_g_2"][0]))
    put("conv_ln_b", cols(inp["conv_ln_b_2"][0]))
    put("pw1_b", cols(inp["conv_pw1_b_2"][0]))
    put("pw2_b", cols(inp["conv_pw2_b_2"][0]))
    for l in range(DEPTH):
        put(f"ln_g{l}", cols(inp["ln_g"][l]))
        put(f"ln_b{l}", cols(inp["ln_b"][l]))
        put(f"ple_b{l}", cols(inp["ple_b_gate"][l]))
        put(f"pos{l}", inp["nsa_pos_k"][l].T, slice(0, 64))
        put(f"pos{l}", inp["nsa_pos_v"][l].T, slice(64, 128))
        put(f"fox_b{l}", inp["fox_b_f"][l][:, None], slice(0, 8))
        put(f"lam{l}", np.broadcast_to(inp["diff_lambda"][l].reshape(1, 128), (P, 128)))
        put(f"subln{l}", np.broadcast_to(inp["diff_subln_g"][l][None], (P, 64)))
        put(f"ada_b{l}", cols(inp["ada_b_2"][l]))
        put(f"norm_g{l}", cols(inp["norm_g_2"][l]))
    return c


def by_k(w):
    return w.reshape(-1, P, w.shape[1]).transpose(1, 0, 2)


def stream():
    def ffn(key):
        yield from (("up", key, t, 4, False) for t in range(FT))
        yield from (("down", key, t, 2, False) for t in range(FT))

    def tiles(key, n):
        yield from (("tile", key, t, 2, False) for t in range(n))

    fills = [("ada", l, g, 8, True) for l in range(DEPTH) for g in range(GROUPS)][::-1]

    for l in range(DEPTH):
        yield from ffn(("ffn1", l))
        yield fills.pop()
        yield fills.pop()
        yield from (("tile", ("w_in", l), t, 2, t == T_FORGET) for t in range(18))
        yield from (("values", ("w_v", l), t, 4, False) for t in range(3))
        yield ("phi", l, 0, 16, True)
        yield ("tile", ("w_v", l), 6, 2, False)
        yield ("phi2", l, 0, 2, True)
        yield fills.pop()
        yield fills.pop()
        yield from tiles(("w_out", l), KT)
        yield fills.pop()
        yield fills.pop()
        yield from ffn(("ffn2", l))
        yield fills.pop()
        yield fills.pop()
        yield from tiles(("ple", l), KT)
        yield ("ple_proj", l, 0, 4, True)
        yield fills.pop()
    for l in range(DEPTH):
        def norm():
            if l == 0:
                yield fills.pop()
                yield fills.pop()
        yield fills.pop()
        yield from norm()
        yield from ffn(("ffn1_2", l))
        yield from norm()
        if l == 0:
            for t in range(KT):
                yield ("up", ("conv", 0), t, 4, False)
                yield fills.pop()
            yield fills.pop()
            yield fills.pop()
            yield from tiles(("pw2", 0), KT)
        else:
            yield from tiles(("qk", 0), 10)
            yield ("values", ("v", 0), 0, 4, False)
            yield from tiles(("wo", 0), KT)
        yield from norm()
        yield from ffn(("ffn2_2", l))
    assert not fills


def raw_quarters():
    return [raw for _, _, _, n, raw in stream() for _ in range(n)]


def lay_weights(inp):
    def matrix(key):
        kind, l = key
        if kind == "w_in":
            w = inp["w_in"][l]
            split = np.cumsum([256, 384, 12, 256, 256, 256, 512, 512, 512, 8])
            nq, nkv, gates, dq, dk, dv, fq, fk, fv, ff = np.split(w, split[:-1], axis=1)
            kv = [nkv[:, 64 * n:64 * n + 64] for n in range(6)]
            last = np.zeros((D, P), np.float32)
            last[:, 0:8], last[:, 32:44] = ff, gates
            return np.concatenate([kv[0], kv[1], kv[2], kv[2], kv[4], kv[4], last, nq, dq, dk, fq, fk], axis=1)
        if kind == "w_v":
            w = inp["w_in"][l]
            return np.concatenate([w[:, 448:512], w[:, 576:640], w[:, 1164:1420], w[:, 2444:2956]], axis=1)
        if kind == "w_out":
            return inp["w_out"][l]
        if kind == "ple":
            return inp["ple_w_gate"][l]
        if kind == "pw2":
            return inp["conv_pw2_w_2"][0]
        if kind == "wo":
            return inp["attn_w_o_2"][0]
        w = inp["attn_w_qkv_2"][0]
        if kind == "v":
            return w[:, D + 256:D + 512]
        q = w[:, :D].reshape(D, 2, 2, 4, 64).transpose(0, 1, 3, 2, 4).reshape(D, D)
        return np.concatenate([q, w[:, D:D + 256]], axis=1)

    def gate_up(key):
        kind, l = key
        if kind in ("ffn1", "ffn2"):
            out = []
            for n in ("gate", "up"):
                w = np.zeros((D, FF), np.float32)
                a = inp[f"{kind}_w_{n}"][l]
                w[:, :a.shape[1]] = a
                out.append(w)
            return out
        w = inp["conv_pw1_w_2"][0] if kind == "conv" else inp[f"{kind[:4]}_wi_2"][l]
        h = w.shape[1] // 2
        return [w[:, :h], w[:, h:]]

    def down(key):
        kind, l = key
        if kind in ("ffn1", "ffn2"):
            w = np.zeros((FF, D), np.float32)
            a = inp[f"{kind}_w_down"][l]
            w[:a.shape[0]] = a
            return w
        return inp[f"{kind[:4]}_wo_2"][l]

    items = list(stream())
    total = sum(n for *_, n, _ in items)
    out = np.zeros((total, P, Q), np.float32)
    at = 0
    held = {}

    def once(what, key, make):
        if held.get(what, (None,))[0] != key:
            held[what] = (key, make())
        return held[what][1]

    for kind, key, t, n, _ in items:
        if kind == "up":
            g, u = once("up", key, lambda: [by_k(w) for w in gate_up(key)])
            parts = [g[:, :, t * P:t * P + P].reshape(P, -1), u[:, :, t * P:t * P + P].reshape(P, -1)]
        elif kind == "down":
            parts = [once("down", key, lambda: by_k(down(key)))[:, t]]
        elif kind == "tile":
            parts = [once("tile", key, lambda: by_k(matrix(key)))[:, :, t * P:t * P + P].reshape(P, -1)]
        elif kind == "values":
            parts = [once("values", key, lambda: by_k(matrix(key)))[:, :, 2 * t * P:2 * t * P + 2 * P].reshape(P, -1)]
        elif kind == "ada":
            parts = [once("ada", key, lambda: by_k(inp["ada_w_2"][key]))[:, :, t * Q:t * Q + Q].reshape(P, -1)]
        elif kind == "phi":
            parts = [np.concatenate([inp[m][key].reshape(CMP_BLOCK, 64, HID).transpose(1, 0, 2)
                                     for m in ("nsa_phi_k1", "nsa_phi_v1")], axis=0).reshape(P, -1)]
        elif kind == "phi2":
            k2, v2 = by_k(inp["nsa_phi_k2"][key]), by_k(inp["nsa_phi_v2"][key])
            parts = [np.concatenate([k2, k2], axis=2).reshape(P, -1), np.zeros((P, Q - 2 * P), np.float32), v2.reshape(P, -1)]
        else:
            parts = [by_k(inp["ple_w_proj"][key]).reshape(P, -1)]
        a = np.concatenate(parts, axis=1) if len(parts) > 1 else parts[0]
        for q in range(n):
            piece = a[:, q * Q:q * Q + Q]
            if piece.shape[1]:
                out[at + q, :, 0:piece.shape[1]] = piece
        at += n
    return out


def lay_rows(x):
    return np.ascontiguousarray(x[0].T.reshape(KT, P, S).transpose(1, 0, 2))


class Seen:

    def __init__(self):
        self.at = {}

    def __call__(self, sem, n=1):
        self.at[sem.name] = self.at.get(sem.name, 0) + n
        return self.at[sem.name]

    def now(self, sem):
        return self.at.get(sem.name, 0)


def build(nc, weights, consts, x_in, ctx_in, p_in, out, n_quarters):
    place, width = columns()
    RAW = raw_quarters()
    FILLS = DEPTH * GROUPS
    with ExitStack() as stack:
        def sb(name, shape, dt=F32):
            return stack.enter_context(nc.sbuf_tensor(name, shape, dt))

        def sem(name):
            return stack.enter_context(nc.semaphore(name))

        ps = stack.enter_context(nc.psum_tensor("ps", [P, 8, 512], F32))
        raw = sb("raw", [P, RING, Q])
        high = sb("high", [P, RING, Q])
        low = sb("low", [P, RING, Q])
        hidden = sb("hidden", [P, FT, 512])
        h_split = sb("h_split", [P, 2, 2, 512])
        x = sb("x", [P, KT, 512])
        zh = sb("zh", [P, KT, 512])
        zl = sb("zl", [P, KT, 512])
        cst = sb("cst", [P, width])
        ple_p = sb("ple_p", [P, DEPTH, 2, S])
        gated = sb("gated", [P, 2, 512])
        std = sb("std", [P, 512])
        row_buf = sb("row_buf", [2, Q])
        mods_raw = sb("mods_raw", [P, NMOD, KT, 2])
        mods = sb("mods", [P, NMOD, KT, 2])
        mod_a = sb("mod_a", [P, 3, KT, 2])
        cs = sb("cs", [P, KT, 2])
        block_kv = sb("block_kv", [P, CMP_BLOCK, 2 * NC])
        hid = sb("hid", [P, 2, 2 * NC])
        hid4 = sb("hid4", [P, 2, 4, PITCH])
        kc = sb("kc", [P, NC])
        kc_t = sb("kc_t", [P, NC])
        vc_diag = sb("vc_diag", [P, 4 * 64])
        sc = sb("sc", [P, ST, 4, PITCH])
        cmp_m = sb("cmp_m", [P, 8])
        cmp_s = sb("cmp_s", [P, 8])
        gates = sb("gates", [P, ST, 12])
        lam_t = sb("lam_t", [P, 64])
        lam_s = sb("lam_s", [P, 4])
        subg = sb("subg", [P, 64])
        neg_max = sb("neg_max", [P, 32, 2])
        sums = sb("sums", [P, 32, 2])
        coef = sb("coef", [P, 32, 2])
        sink_e = sb("sink_e", [P, 32])
        rms = sb("rms", [P, 8])
        rstd = std

        def carve_of(flat, start, *shape):
            n = int(np.prod(shape))
            names = " ".join("abcd"[:len(shape)])
            return flat[:, start:start + n].rearrange(f"p ({names}) -> p {names}", **dict(zip("abcd", shape)))

        def carve(start, *shape):
            return carve_of(hidden[:].rearrange("p a b -> p (a b)"), start, *shape)

        proj = carve(0, 18, S)
        val = carve(4608, ST, V_ALL)
        probs = carve(6400, 3, 512)
        probs_t = carve(7936, 2, 512)
        heads = carve(8960, ST, D)
        forget = carve(11008, S)[0:8]
        fl = carve(6400, 4, S)[0:8]
        hid_r = carve(7424, S)[0:2 * NC]
        pc_t = carve(7680, ST, P)
        tmp = gated
        square = hidden
        wide = hidden[:, KT:2 * KT, :]
        conv_in = carve(0, KT, 2, S + 2 * PAD)
        conv_out = carve(KT * 2 * (S + 2 * PAD), KT, 512)
        q_at = carve(0, KT, S)
        k_at = carve(2048, 2, 512)
        v_at = carve(3072, 4, 256)

        def c(name, rows=slice(0, P)):
            s, w = place[name]
            return cst[rows, s:s + w]

        def r(ap):
            return ap.bitcast(F32R)

        landed = [sem(f"quarter_landed{i}") for i in range(RING)]
        x_landed = sem("x_landed")
        consts_landed = sem("consts_landed")
        rest_landed = sem("rest_landed")
        quarter_done = sem("quarter_done")
        high_ready = sem("high_ready")
        low_ready = sem("low_ready")
        silu_ready = sem("silu_ready")
        hidden_ready = sem("hidden_ready")
        h_high = sem("h_high")
        h_low = sem("h_low")
        z_ready = sem("z_ready")
        stat_ready = sem("stat_ready")
        dev_ready = sem("dev_ready")
        sq_ready = sem("sq_ready")
        std_ready = sem("std_ready")
        scaled_ready = sem("scaled_ready")
        norm_ready = sem("norm_ready")
        in_ready = sem("in_ready")
        sig_ready = sem("sig_ready")
        res_ready = sem("res_ready")
        dve_step = sem("dve_step")
        act_step = sem("act_step")
        stored = sem("stored")
        result_ready = sem("result_ready")
        proj_ready = sem("proj_ready")
        val_ready = sem("val_ready")
        conv_taken = sem("conv_taken")
        gates_ready = sem("gates_ready")
        swapped = sem("swapped")
        rope_ready = sem("rope_ready")
        blocks_ready = sem("blocks_ready")
        gelu_ready = sem("gelu_ready")
        hid_turned = sem("hid_turned")
        hid_ready = sem("hid_ready")
        hid4_ready = sem("hid4_ready")
        kc_raw = sem("kc_raw")
        kc_swapped = sem("kc_swapped")
        kc_ready = sem("kc_ready")
        forget_in = sem("forget_in")
        forget_act = sem("forget_act")
        forget_ready = sem("forget_ready")
        lam_in = sem("lam_in")
        lam_act = sem("lam_act")
        cmp_scores = sem("cmp_scores")
        cmp_in = sem("cmp_in")
        cmp_exp = sem("cmp_exp")
        cmp_probs = sem("cmp_probs")
        cmp_turned = sem("cmp_turned")
        cmp_t = sem("cmp_t")
        cmp_out = sem("cmp_out")
        score_ready = sem("score_ready")
        max_ready = sem("max_ready")
        exp_done = sem("exp_done")
        sink_ready = sem("sink_ready")
        turned = sem("turned")
        probs_t_ready = sem("probs_t_ready")
        out_ready = sem("out_ready")
        out_taken = sem("out_taken")
        rms_in = sem("rms_in")
        rms_act = sem("rms_act")
        heads_whole = sem("heads_whole")
        heads_turned = sem("heads_turned")
        heads_ready = sem("heads_ready")
        mods_ready = sem("mods_ready")
        cs_ready = sem("cs_ready")
        rows_ready = sem("rows_ready")
        rows_taken = sem("rows_taken")
        rows_turned = sem("rows_turned")
        cols_taken = sem("cols_taken")

        block = stack.enter_context(nc.Block())

        def stages(e):
            e.start()
            e.split_x(S)
            for l in range(DEPTH):
                e.ffn(S)
                e.post_norm(2 * ALPHA, 0, c(f"ln_g{l}")[:, 0:KT], c(f"ln_b{l}")[:, 0:KT])
                e.mixer(l)
                e.post_norm(ALPHA, 1, c(f"ln_g{l}")[:, KT:2 * KT], c(f"ln_b{l}")[:, KT:2 * KT])
                e.ffn(S)
                e.post_norm(2 * ALPHA, 0, c(f"ln_g{l}")[:, 2 * KT:3 * KT], c(f"ln_b{l}")[:, 2 * KT:3 * KT])
                e.ple(l)
                if l == 0:
                    e.split_x(S)
            for l in range(DEPTH):
                e.modulation(l)
                e.pre_norm(512, 0, l)
                e.ffn(512)
                e.residual(512, 2)
                e.pre_norm(512, 1, l)
                if l == 0:
                    e.conv()
                    e.residual(512, 5)
                else:
                    e.attention()
                    e.residual(S, 5)
                T = 512 if l == 0 else S
                e.pre_norm(T, 2, l)
                e.ffn(T)
                e.residual(T, 8)
            e.finish()

        def y_tile(T, d):
            return ps[:, d, :] if T == 512 else ps[:, 4 + d // 2, d % 2 * S:d % 2 * S + S]

        def y_bank(b):
            return ps[:, 4 + b, :].rearrange("p (t s) -> p t s", t=2)

        def halves(T):
            return [slice(i, i + S) for i in range(0, T, S)]

        def pieces(T):
            return [(k, h, cols) for k in range(KT) for h, cols in enumerate(halves(T))]

        def mixer_jobs():
            jobs = []
            for t in range(ST):
                for i in range(4):
                    maps = [(T_DQ + n, T_DK + n, 32 * i, 32, V_DIFF + 64 * (2 * n + i // 2), None) for n in range(2)]
                    jobs.append((t, maps, "diff0" if i % 2 == 0 else "diff1", 256 + 64 * (i // 2)))
                for kind, kt, vc in (("slc", T_KSLC, V_SLC), ("win", T_KWIN, V_WIN)):
                    for i in range(2):
                        maps = [(T_NQ + n, kt, 64 * i, 64, vc, None) for n in range(2)]
                        jobs.append((t, maps, kind, 64 * i))
                for m in range(2):
                    for i in range(2):
                        maps = [(T_FQ + 2 * m + n, T_FK + 2 * m + n, 64 * i, 64, V_FOX + 64 * (4 * m + 2 * n + i),
                                 4 * m + 2 * n + i) for n in range(2)]
                        jobs.append((t, maps, "fox", 512 + 64 * (4 * m + i)))
            return jobs

        JOBS = mixer_jobs()
        JOBS2 = [(t, p, g, i) for t in range(ST) for p in range(2) for g in range(4) for i in range(2)]

        @block.sync
        def _(sp):
            def load(n, source):
                sp.dma_start(raw[:, n, :], source).then_inc(landed[n], 16)

            def slot_free(q, lap=None):
                before = q - RING
                if RAW[before]:
                    sp.wait_ge(quarter_done, before + 1 + RING)
                else:
                    n = sum(not a for a in RAW[:before + 1])
                    sp.wait_ge(low_ready, n if lap is None else lap * RING + n)

            sp.dma_start(x[:, :, 0:S], x_in).then_inc(x_landed, 16)
            load(0, weights[0])
            load(1, weights[1])
            sp.dma_start(cst[:], consts).then_inc(consts_landed, 16)
            for n in range(2, RING):
                load(n, weights[n])
            q = RING
            while q < n_quarters:
                laps = 0
                while q + (laps + 1) * RING <= n_quarters and not any(RAW[q - RING + laps * RING:q + laps * RING]):
                    laps += 1
                if laps >= 2:
                    with sp.Fori(0, laps) as lap:
                        for n in range(RING):
                            slot_free(q + n, lap)
                            load((q + n) % RING, weights[lap * RING + (q + n)])
                    q += laps * RING
                else:
                    slot_free(q)
                    load(q % RING, weights[q])
                    q += 1

        class PE:
            def __init__(self, pe):
                self.pe, self.seen = pe, Seen()
                self.q = 0
                self.split = 0
                self.fills = 0
                self.turns = 0

            def start(self):
                pass

            def split_x(self, T):
                pass

            def input_waits(self, T):
                for k in range(KT):
                    self.pe.wait_ge(in_ready, self.seen(in_ready, T // S))
                    yield k

            def whole_input(self, T):
                for _ in self.input_waits(T):
                    pass

            def coming_input(self, T):
                return [self.seen(in_ready, T // S) for _ in range(KT)]

            def mm(self, out, lhsT, rhs, first, last, **kw):
                return nc.tensor.matmul(out, lhsT, rhs, start=first, stop=last, **kw)

            def mm3(self, out, lhsT, rhs, first, last, **kw):
                self.mm(out, r(lhsT[1]), r(rhs[0]), first, False, **kw)
                self.mm(out, r(lhsT[0]), r(rhs[1]), False, False, **kw)
                return self.mm(out, r(lhsT[0]), r(rhs[0]), False, last, **kw)

            def z(self, k, cols):
                return zh[:, k, cols], zl[:, k, cols]

            def quarter(self, lap=None):
                q, lo = self.q, self.split + 1
                assert not RAW[q]
                self.pe.wait_ge(low_ready, lo if lap is None else lap * (4 * STEPS) + lo)
                self.q += 1
                self.split += 1
                return high[:, q % RING, :], low[:, q % RING, :]

            def raw_quarter(self):
                q = self.q
                assert RAW[q]
                self.pe.wait_ge(landed[q % RING], 16 * (q // RING + 1))
                self.q += 1
                return raw[:, q % RING, :]

            def done(self, mm):
                mm.then_inc(quarter_done, 1)

            def tile(self, o, T, lap=None, coming=None):
                for a in range(2):
                    h, lo = self.quarter(lap)
                    for i in range(4):
                        k = 4 * a + i
                        w = (h[:, i * P:i * P + P], lo[:, i * P:i * P + P])
                        if coming:
                            self.pe.wait_ge(in_ready, coming[k])
                        m = self.mm3(o, w, self.z(k, slice(0, T)), k == 0, k == KT - 1)
                    self.done(m)

            def ffn(self, T):
                pe = self.pe
                h0 = self.seen(hidden_ready, RING if self.seen.now(hidden_ready) == 0 else 0)
                coming = self.coming_input(T)
                ways = 2 if T == 512 else 4
                q0, s0 = self.q, self.split
                with pe.Fori(0, LOOPS) as i:
                    for j in range(STEPS):
                        prev = j - ways if j >= ways else max(n for n in range(STEPS) if n % ways == j) - STEPS
                        pe.wait_ge(hidden_ready, i * STEPS + (h0 + prev + 1))
                        for g in range(2):
                            self.tile(ps[:, 2 * (j % 2) + g, :] if T == 512 else ps[:, j % 4, g * S:g * S + S], T, i,
                                      coming if j == 0 and g == 0 else None)
                self.q, self.split = q0 + 4 * FT, s0 + 4 * FT
                pe.wait_ge(hidden_ready, self.seen(hidden_ready, FT))
                self.fills_out()
                for f in range(FT):
                    pe.wait_ge(h_low, self.seen(h_low))
                    hs = (h_split[:, f % 2, 0, 0:T], h_split[:, f % 2, 1, 0:T])
                    for a in range(2):
                        h, lo = self.quarter()
                        for i in range(4):
                            d = 4 * a + i
                            w = (h[:, i * P:i * P + P], lo[:, i * P:i * P + P])
                            m = self.mm3(y_tile(T, d), w, hs, f == 0 and (T == 512 or d % 2 == 0), f == FT - 1,
                                         skip_group_check=True)
                        self.done(m)

            def stats(self, T, bank, ready, per, src):
                for k in range(KT):
                    if k % 2 == 0:
                        self.pe.wait_ge(ready, self.seen(ready, per))
                    m = self.mm(ps[:, bank, 0:T], c("mean"), src[:, k, 0:T], k == 0, k == KT - 1)
                m.then_inc(stat_ready, 1)

            def turn_rows(self, bank):
                if self.turns == self.fills:
                    return
                if self.turns:
                    self.pe.wait_ge(cols_taken, self.turns)
                self.turns += 1
                self.pe.wait_ge(rows_taken, self.turns)
                for i in range(4):
                    m = nc.tensor.transpose(ps[:, bank, 2 * i:2 * i + 2], row_buf[:, i * P:i * P + P], c("ident", slice(0, 2))[:, 0:2])
                m.then_inc(rows_turned, 1)

            def fill(self, rows=4, cols=6):
                self.turn_rows(cols)
                if self.fills == 0:
                    self.pe.wait_ge(cs_ready, 1)
                for k in range(KT):
                    w = self.raw_quarter()
                    self.done(self.mm(ps[0:2, rows, :], cs[:, k, :], w, k == 0, k == KT - 1))
                self.fills += 1

            def fills_out(self):
                if self.fills:
                    self.pe.wait_ge(rows_taken, self.fills)
                if self.turns:
                    self.pe.wait_ge(cols_taken, self.turns)

            def post_norm(self, scale, eps, g, b):
                self.pe.wait_ge(consts_landed, 16)
                self.stats(S, 0, z_ready, 1, wide)
                self.fill()
                self.stats(S, 1, sq_ready, 1, square)
                self.fill()

            def pre_norm(self, T, n, l):
                if l == 0:
                    if n > 0:
                        self.pe.wait_ge(res_ready, self.seen.now(res_ready) + 6)
                        self.seen(res_ready, 2 * KT)
                    self.fill(1, 2)
                self.stats(T, 0, sq_ready, 1, square)
                if l == 0:
                    self.fill()

            def modulation(self, l):
                self.pe.wait_ge(res_ready, self.seen(res_ready, 4 if l == 0 else 2 * KT))
                if l == 0:
                    self.turn_rows(6)
                    self.fills_out()
                    self.fill()
                else:
                    self.fill()
                    self.turn_rows(6)

            def ple(self, l):
                self.pe.wait_ge(rest_landed, 32)
                coming = self.coming_input(S)
                for d in range(KT):
                    if d >= 4:
                        self.pe.wait_ge(sig_ready, self.seen.now(sig_ready) + d - 3)
                    self.tile(ps[:, d % 4, d // 4 * S:d // 4 * S + S], S, coming=coming if d == 0 else None)
                self.seen(sig_ready, KT)
                self.fills_out()
                for k in range(2):
                    for a in range(2):
                        w = self.raw_quarter()
                        for i in range(4):
                            d = 4 * a + i
                            m = self.mm(y_tile(S, d), w[:, i * P:i * P + P], ple_p[:, l, k, :], k == 0 and d % 2 == 0, k == 1,
                                        skip_group_check=True)
                        self.done(m)
                self.pe.wait_ge(res_ready, self.seen.now(res_ready) + 4)
                if l == 0:
                    self.seen(res_ready, 4)
                self.fill()

            def mixer(self, l):
                pe, seen = self.pe, self.seen
                coming = self.coming_input(S)
                pr0 = seen.now(proj_ready)
                for n in range(9):
                    if n >= 4:
                        pe.wait_ge(proj_ready, pr0 + n - 3)
                    for d in range(2):
                        o = ps[:, n % 4, d * S:d * S + S]
                        if 2 * n + d != T_FORGET:
                            self.tile(o, S, coming=coming if n == 0 and d == 0 else None)
                            continue
                        w = [self.raw_quarter(), self.raw_quarter()]
                        wk = [w[k // 4][:, k % 4 * P:k % 4 * P + P] for k in range(KT)]
                        for k in range(KT):
                            self.mm(o[0:8, :], wk[k][:, 0:8], x[:, k, 0:S], k == 0, k == KT - 1)
                        for t in range(ST):
                            for k in range(KT):
                                m = self.mm(ps[:, 7, 12 * t:12 * t + 12], x[:, k, t * P:t * P + P], wk[k][:, 32:44], k == 0, k == KT - 1)
                                if t == ST - 1 and k == KT - 2:
                                    self.done(m)
                        self.done(m)
                for n in range(3):
                    pe.wait_ge(proj_ready, pr0 + 9 + n - 3)
                    self.values(ps[:, (9 + n) % 4, :], range(ST))
                pe.wait_ge(proj_ready, seen(proj_ready, 9))
                pe.wait_ge(gates_ready, seen(gates_ready))
                self.fills_out()
                for bank, (t, swap) in zip((4, 5, 6, 7), ((T_KSLC, "swap64"), (T_NQ, "swap64"), (T_DQ, "swap32"), (T_DK, "swap32"))):
                    self.mm(ps[:, bank, :], c(swap), proj[:, t:t + 2, :], True, True).then_inc(swapped, 1)
                pe.wait_ge(blocks_ready, seen(blocks_ready, 2))
                for n in range(CMP_BLOCK // 2):
                    w = self.raw_quarter()
                    for i in range(2):
                        m = self.mm(ps[0:2 * NC, 0, 0:HID], block_kv[:, 2 * n + i, :], w[:, i * HID:i * HID + HID],
                                    n == 0 and i == 0, n == CMP_BLOCK // 2 - 1 and i == 1)
                    self.done(m)
                pe.wait_ge(val_ready, seen(val_ready, 3))
                for a in range(2):
                    h, lo = self.quarter()
                    for t in range(ST):
                        for i in range(4):
                            k = 4 * a + i
                            m = self.mm3(ps[:, 1 + t, 0:P], self.z(k, slice(t * P, t * P + P)), (h[:, i * P:i * P + P], lo[:, i * P:i * P + P]),
                                         k == 0, k == KT - 1)
                    self.done(m)
                pe.wait_ge(gelu_ready, seen(gelu_ready))
                for h in range(2):
                    m = nc.tensor.transpose(ps[:, 0, 2 * NC * h:2 * NC * h + 2 * NC], hid_r[:, h * P:h * P + P], c("ident", slice(0, 2 * NC))[:, 0:2 * NC])
                m.then_inc(hid_turned, 1)
                two = [self.raw_quarter(), self.raw_quarter()]
                wk, wv = two[0][:, 0:256].rearrange("p (h m) -> p h m", h=2), two[1][:, 0:128].rearrange("p (h m) -> p h m", h=2)
                pe.wait_ge(hid_ready, seen(hid_ready))
                for h in range(2):
                    m = self.mm(ps[:, 3, 0:NC], wk[:, h, :], hid[:, h, 0:NC], h == 0, h == 1)
                self.done(m)
                pe.wait_ge(rope_ready, seen(rope_ready, 4))
                pe.wait_ge(hid4_ready, seen(hid4_ready))
                for h in range(2):
                    m = self.mm(ps[:, 5, 0:64], hid4[:, h, :, :].rearrange("p a b -> p (a b)"), wv[:, h, :], h == 0, h == 1)
                self.done(m)
                pe.wait_ge(kc_raw, seen(kc_raw))
                self.mm(ps[:, 4, 0:NC], c("swap64"), kc[:], True, True).then_inc(kc_swapped, 1)
                pe.wait_ge(kc_ready, seen(kc_ready, 2))
                pe.wait_ge(val_ready, seen(val_ready, 1))
                for t in range(ST):
                    for h in (0, 2, 1, 3):
                        q = slice(64 * (h % 2), 64 * (h % 2) + 64)
                        at = (2 * t + h // 2) * 16
                        m = self.mm(ps[:, 5 + h % 2, at:at + NC], proj[q, T_NQ + h // 2, t * P:t * P + P], kc[q, :], True, True)
                m.then_inc(cmp_scores, 1)
                self.fill(0, 1)
                pe.wait_ge(cmp_probs, seen(cmp_probs))
                for t in range(ST):
                    m = nc.tensor.transpose(ps[:, 7, t * P:t * P + P], sc[:, t, :, :].rearrange("p a b -> p (a b)"), c("ident"))
                m.then_inc(cmp_turned, 1)
                self.fill(4, 3)
                pe.wait_ge(cmp_t, seen(cmp_t))
                for t in range(ST):
                    m = self.mm(ps[:, 7, t * 256:t * 256 + 256], pc_t[:, t, :], vc_diag[:], True, True)
                m.then_inc(cmp_out, 1)
                pe.wait_ge(forget_ready, seen(forget_ready))
                self.fills_out()

                def scores(j, bank):
                    t, maps, _, _ = JOBS[j]
                    kw = (t + 1) * P
                    for m, (qt, kt, p0, wd, _, fh) in enumerate(maps):
                        rows = slice(p0, p0 + wd)
                        at = m * S
                        self.mm(ps[:, bank, at:at + kw], proj[rows, qt, t * P:t * P + P], proj[rows, kt, 0:kw],
                                True, False, skip_group_check=True)
                        if fh is not None:
                            self.mm(ps[:, bank, at:at + kw], c("ident", slice(0, 8))[:, fh:fh + 1].broadcast_to([8, P]), forget[:, 0:kw],
                                    False, False, skip_group_check=True)
                        o = self.mm(ps[:, bank, at + t * P:at + kw], c("ident"), c("low"), False, True, skip_group_check=True)
                    o.then_inc(score_ready, 1)

                def blocks(j):
                    t, maps, _, _ = JOBS[j]
                    return [(m, kb, m * S + kb * P, v) for m, (_, _, _, _, v, _) in enumerate(maps) for kb in range(t + 1)]

                self.jobs(len(JOBS), 2, scores, blocks, lambda j, kb, v: val[:, kb, v:v + 64], lambda j: JOBS[j][0] + 1)
                self.turn_heads()
                self.square_product(S)

            def values(self, o, rows):
                for a in range(4):
                    h, lo = self.quarter()
                    for t in rows:
                        for i in range(2):
                            k = 2 * a + i
                            at = 256 * (t - rows[0])
                            m = self.mm3(o[:, at:at + 256], self.z(k, slice(t * P, t * P + P)), (h[:, i * 256:i * 256 + 256], lo[:, i * 256:i * 256 + 256]),
                                         k == 0 and at == 0, k == KT - 1, skip_group_check=True)
                    self.done(m)

            def jobs(self, n, maps, scores, blocks, v_of, kbs):
                pe, seen = self.pe, self.seen
                e0, p0, o0 = seen.now(exp_done), seen.now(probs_t_ready), seen.now(out_taken)
                for j in range(n + 2):
                    if j < n:
                        if j >= 3:
                            pe.wait_ge(exp_done, e0 + maps * (j - 2))
                        scores(j, j % 3)
                    if 1 <= j <= n:
                        a = j - 1
                        pe.wait_ge(exp_done, e0 + maps * (a + 1))
                        if a >= 2:
                            pe.wait_ge(probs_t_ready, p0 + a - 1)
                        for i, (m, kb, at, v) in enumerate(blocks(a)):
                            o = nc.tensor.transpose(ps[:, 3 + a % 2, i * P:i * P + P], probs[:, a % 3, at:at + P], c("ident"))
                        o.then_inc(turned, 1)
                    if j >= 2:
                        a = j - 2
                        pe.wait_ge(probs_t_ready, p0 + a + 1)
                        if a >= 2:
                            pe.wait_ge(out_taken, o0 + a - 1)
                        for i, (m, kb, at, v) in enumerate(blocks(a)):
                            o = self.mm(ps[:, 5 + a % 2, m * 64:m * 64 + 64], probs_t[:, a % 2, i * P:i * P + P], v_of(a, kb, v),
                                        kb == 0, kb == kbs(a) - 1)
                        o.then_inc(out_ready, 1)
                seen(exp_done, maps * n), seen(probs_t_ready, n), seen(out_taken, n)

            def turn_heads(self):
                pe, seen = self.pe, self.seen
                pe.wait_ge(heads_whole, seen(heads_whole))
                for t in range(ST):
                    for b in range(2):
                        for i in range(4):
                            o = nc.tensor.transpose(ps[:, 2 * t + b, i * P:i * P + P], heads[:, t, (4 * b + i) * P:(4 * b + i) * P + P], c("ident"))
                        o.then_inc(heads_turned, 1)
                pe.wait_ge(in_ready, seen(in_ready, 4))

            def square_product(self, T, coming=None):
                for d in range(KT):
                    self.tile(y_tile(T, d), T, coming=coming if d == 0 else None)

            def residual(self, T, g):
                pass

            def conv(self):
                pe, seen = self.pe, self.seen
                coming = self.coming_input(512)
                for n in range(KT):
                    if n >= 2:
                        pe.wait_ge(conv_taken, seen.now(conv_taken) + n - 1)
                    for g in range(2):
                        self.tile(ps[:, 2 * (n % 2) + g, :], 512, coming=coming if n == 0 and g == 0 else None)
                    self.fill(6, 7)
                seen(conv_taken, KT)
                self.stats(512, 0, z_ready, 2, conv_out)
                self.fill(6, 7)
                self.stats(512, 1, sq_ready, 1, square)
                self.fill(6, 7)
                coming = self.coming_input(S)
                self.fills_out()
                self.square_product(512, coming)

            def attention(self):
                pe, seen = self.pe, self.seen
                pe.wait_ge(res_ready, seen(res_ready, 2 * KT))
                self.fills_out()
                self.whole_input(512)
                pr0 = seen.now(proj_ready)
                for n in range(10):
                    o = ps[:, n // 2, n % 2 * S:n % 2 * S + S] if n < 8 else ps[:, 4 + n % 2, :]
                    self.tile(o, S if n < 8 else 512)
                for i in range(2):
                    pass
                for a in range(4):
                    h, lo = self.quarter()
                    for t in range(4):
                        for i in range(2):
                            k = 2 * a + i
                            m = self.mm3(ps[:, 6 + t // 2, 256 * (t % 2):256 * (t % 2) + 256], self.z(k, slice(t * P, t * P + P)),
                                         (h[:, i * 256:i * 256 + 256], lo[:, i * 256:i * 256 + 256]), k == 0 and t % 2 == 0, k == KT - 1,
                                         skip_group_check=True)
                    self.done(m)
                pe.wait_ge(proj_ready, seen(proj_ready, 6))
                for n in range(4):
                    self.mm(ps[:, n, :], c("swapax"), q_at[:, 2 * n:2 * n + 2, :], True, True).then_inc(swapped, 1)
                self.mm(ps[:, 4, :], c("swapax"), k_at[:, :, 0:S], True, True).then_inc(swapped, 1)
                pe.wait_ge(val_ready, seen(val_ready, 1))
                pe.wait_ge(rope_ready, seen(rope_ready, 5))

                def scores(j, bank):
                    t, p, g, i = JOBS2[j]
                    rows = slice(64 * i, 64 * i + 64)
                    self.mm(ps[:, bank, :], q_at[rows, 4 * p + g, t * P:t * P + P], k_at[rows, p, :], True, False, skip_group_check=True)
                    o = self.mm(ps[:, bank, P:2 * P] if t == 0 else ps[:, bank, 0:P], c("ident"), c("low" if t == 0 else "high"),
                                False, True, skip_group_check=True)
                    o.then_inc(score_ready, 1)

                def v_of(j, kb, v):
                    t, p, g, i = JOBS2[j]
                    return v_at[:, kb, 64 * (2 * p + i):64 * (2 * p + i) + 64]

                self.jobs(len(JOBS2), 1, scores, lambda j: [(0, kb, kb * P, None) for kb in range(4)], v_of, lambda j: 4)
                self.turn_heads()
                self.square_product(S)

            def finish(self):
                self.stats(S, 0, sq_ready, 1, square)

        @block.tensor
        def _(pe):
            stages(PE(pe))

        class Act:
            def __init__(self, act):
                self.act, self.seen = act, Seen()
                self.q = 0
                self.s = 0
                self.n = 0
                self.fills = 0
                self.taken = 0

            def f(self, out, in_, func, **kw):
                return nc.scalar.activation(out, in_, func, **kw)

            def start(self):
                self.act.wait_ge(x_landed, 16)

            def high(self, lap=None):
                q, act = self.s, self.act
                self.s += 1
                if q >= len(RAW) or RAW[q]:
                    return
                self.n += 1
                at = 16 * (q // RING + 1)
                act.wait_ge(landed[q % RING], at if lap is None else lap * (16 * 4) + at)
                at = q - RING + 1 + RING
                act.wait_ge(quarter_done, at if lap is None else lap * (4 * STEPS) + at)
                self.f(r(high[:, q % RING, :]), raw[:, q % RING, :], ACT.Copy).then_inc(high_ready, 1)

            def ahead(self, n=0):
                while self.s < self.q + n + AHEAD:
                    self.high()

            def used(self, n):
                self.ahead(n)
                self.q += n
                self.act.wait_ge(quarter_done, self.q + RING)

            def split_x(self, T):
                if self.q:
                    self.ahead()
                for k in range(KT):
                    if self.q and k % 2 == 0:
                        self.act.wait_ge(res_ready, self.seen(res_ready))
                    self.f(r(zh[:, k, 0:T]), x[:, k, 0:T], ACT.Copy).then_inc(norm_ready, 1)
                if not self.q:
                    self.ahead()
                    self.act.wait_ge(consts_landed, 16)
                    self.f(cs[:].rearrange("p k c -> p (k c)"), c("csil"), ACT.Silu).then_inc(cs_ready, 1)

            def ffn(self, T):
                act, seen = self.act, self.seen
                h0 = seen(hidden_ready, RING if seen.now(hidden_ready) == 0 else 0)
                self.ahead()
                self.take_rows()
                s0, n0, q0 = self.s, self.n, self.q
                with act.Fori(0, LOOPS) as i:
                    for j in range(STEPS):
                        for _ in range(4):
                            self.high(i)
                        act.wait_ge(quarter_done, i * (4 * STEPS) + (q0 + 4 * (j + 1) + RING))
                        prev = j - 2 if j >= 2 else (STEPS - 1 if j == 0 else STEPS - 2) - STEPS
                        act.wait_ge(hidden_ready, i * STEPS + (h0 + prev + 1))
                        g = ps[:, 2 * (j % 2), :] if T == 512 else ps[:, j % 4, 0:S]
                        self.f(gated[:, j % 2, 0:T], g, ACT.Silu).then_inc(silu_ready, 1)
                self.s, self.n, self.q = s0 + 4 * FT, n0 + 4 * FT, q0 + 4 * FT
                for f in range(FT):
                    act.wait_ge(hidden_ready, seen(hidden_ready))
                    if f >= 2:
                        act.wait_ge(quarter_done, self.q + 2 * (f - 1) + RING)
                    self.f(r(h_split[:, f % 2, 0, 0:T]), hidden[:, f, 0:T], ACT.Copy).then_inc(h_high, 1)
                    while self.s < self.q + 2 * (f - 1) + AHEAD:
                        self.high()
                self.q += 2 * FT
                self.ahead()

            def take_rows(self):
                if self.taken == self.fills:
                    return
                self.act.wait_ge(quarter_done, self.rows_at + RING)
                if self.taken:
                    self.act.wait_ge(rows_turned, self.taken)
                self.taken += 1
                self.f(row_buf[:], ps[0:2, self.rows_bank, :], ACT.Copy).then_inc(rows_taken, 1)

            def fill(self, rows=4, cols=6):
                self.take_rows()
                self.q += KT
                self.rows_at, self.rows_bank = self.q, rows
                self.fills += 1

            def scaled(self, T, func, bias):
                for k, h, cols in pieces(T):
                    self.act.wait_ge(scaled_ready, self.seen(scaled_ready))
                    b = bias(k, h)
                    self.f(r(zh[:, k, cols]), self.src[:, k, cols], func, bias=b)
                    self.f(self.src[:, k, cols], self.src[:, k, cols], func, bias=b).then_inc(norm_ready, 1)

            def post_norm(self, scale, eps, g, b):
                act, seen = self.act, self.seen
                self.fill()
                for k in range(0, KT, 2):
                    act.wait_ge(dev_ready, seen(dev_ready))
                    self.f(square[:, k:k + 2, 0:S], wide[:, k:k + 2, 0:S], ACT.Square).then_inc(sq_ready, 1)
                self.ahead()
                self.take_rows()
                act.wait_ge(stat_ready, seen(stat_ready, 2))
                self.f(std[:, 0:S], ps[:, 1, 0:S], ACT.Sqrt, bias=c("eps")[:, eps:eps + 1]).then_inc(std_ready, 1)
                self.fill()
                self.src = x
                self.scaled(S, ACT.Identity, lambda k, h: b[:, k:k + 1])
                self.ahead()

            def pre_norm(self, T, n, l):
                act, seen = self.act, self.seen
                if l == 0:
                    self.fill(1, 2)
                for k in range(0, KT, 2):
                    act.wait_ge(res_ready, seen(res_ready, self.res_per))
                    self.f(square[:, k:k + 2, 0:T], x[:, k:k + 2, 0:T], ACT.Square).then_inc(sq_ready, 1)
                self.take_rows()
                self.ahead()
                act.wait_ge(stat_ready, seen(stat_ready))
                self.f(std[:, 0:T], ps[:, 0, 0:T], ACT.Sqrt, bias=c("eps")[:, 2:3]).then_inc(std_ready, 1)
                if l == 0:
                    self.fill()
                act.wait_ge(mods_ready, seen(mods_ready, 1 if n == 0 else 0))
                self.src = wide
                self.scaled(T, ACT.Identity, lambda k, h: mods[:, 3 * n, k, h:h + 1])
                self.ahead()

            def modulation(self, l):
                self.act.wait_ge(rest_landed, 32)
                self.fill()
                if l > 0:
                    self.take_rows()

            def ple(self, l):
                self.ahead(2)
                self.take_rows()
                for d in range(KT):
                    self.used(2)
                    self.f(square[:, d, 0:S], ps[:, d % 4, d // 4 * S:d // 4 * S + S], ACT.Sigmoid,
                           bias=c(f"ple_b{l}")[:, d:d + 1]).then_inc(sig_ready, 1)
                self.q += 4
                self.res_per = 1
                self.fill()
                if l == DEPTH - 1:
                    return

            def mixer(self, l):
                act, seen = self.act, self.seen
                self.ahead(4)
                self.take_rows()
                for n in range(9):
                    self.used(4)
                    if n == 1:
                        self.f(proj[:, 2, :], ps[:, 1, 0:S], ACT.Copy)
                        self.f(proj[0:8, 3, :], ps[0:8, 1, S:512], ACT.Copy).then_inc(proj_ready, 1)
                        self.f(gates[:], ps[:, 7, 0:24], ACT.Sigmoid).then_inc(gates_ready, 1)
                    else:
                        self.f(proj[:, 2 * n:2 * n + 2, :], ps[:, n % 4, :], ACT.Copy, scale=PROJ_SCALE[n]).then_inc(proj_ready, 1)
                self.ahead(4)
                act.wait_ge(forget_in, seen(forget_in))
                self.f(fl[:, 0, :], fl[:, 3, :], ACT.Abs).then_inc(act_step, 1)
                act.wait_ge(act_step, seen(act_step))
                self.f(fl[:, 1, :], fl[:, 0, :], ACT.Exp, scale=-1.0).then_inc(act_step, 1)
                act.wait_ge(act_step, seen(act_step))
                self.f(fl[:, 1, :], fl[:, 1, :], ACT.Ln, bias=c("eps", slice(0, 8))[:, 3:4]).then_inc(forget_act, 1)
                act.wait_ge(lam_in, seen(lam_in))
                self.f(lam_s[:, 0:2], lam_s[:, 0:2], ACT.Exp).then_inc(lam_act, 1)
                self.used(12)
                self.used(16)
                self.f(hid_r, ps[0:2 * NC, 0, 0:HID], ACT.Gelu_apprx_tanh).then_inc(gelu_ready, 1)
                act.wait_ge(hid_turned, seen(hid_turned))
                self.f(hid[:].rearrange("p a b -> p (a b)"), ps[:, 0, 0:4 * NC], ACT.Copy).then_inc(hid_ready, 1)
                self.used(3)
                self.f(kc[:], ps[:, 3, 0:NC], ACT.Copy).then_inc(kc_raw, 1)
                self.q += 1
                act.wait_ge(cmp_in, seen(cmp_in))
                self.f(sc[:].rearrange("p t h c -> p (t h) c")[:, :, 0:NC], sc[:].rearrange("p t h c -> p (t h) c")[:, :, 0:NC],
                       ACT.Exp).then_inc(cmp_exp, 1)
                self.fill(0, 1)
                act.wait_ge(cmp_turned, seen(cmp_turned))
                self.f(pc_t.rearrange("p t q -> p (t q)"), ps[:, 7, 0:S], ACT.Copy).then_inc(cmp_t, 1)
                self.take_rows()
                self.fill(4, 3)
                self.ahead()
                self.take_rows()

                def exps(j, b):
                    t, maps, _, _ = JOBS[j]
                    for m in range(2):
                        self.f(probs[:, b, m * S:m * S + (t + 1) * P], ps[:, b, m * S:m * S + (t + 1) * P], ACT.Exp,
                               bias=neg_max[:, j, m:m + 1], accum_out=sums[:, j, m:m + 1]).then_inc(exp_done, 1)

                self.jobs(len(JOBS), exps)
                act.wait_ge(rms_in, seen(rms_in))
                self.f(rms[:], rms[:], ACT.Sqrt, bias=c("eps")[:, 1:2], scale=1.0 / 64).then_inc(rms_act, 1)
                self.turn_heads()
                self.last_product()

            def last_product(self):
                self.ahead(4)
                for n in range(4, 16, 4):
                    self.act.wait_ge(quarter_done, self.q + n + RING)
                    self.ahead(n + 4)
                self.q += 2 * KT

            def jobs(self, n, exps):
                act, seen = self.act, self.seen
                m0, t0 = seen.now(max_ready), seen.now(turned)
                for j in range(n):
                    act.wait_ge(max_ready, m0 + j + 1)
                    if j >= 3:
                        act.wait_ge(turned, t0 + j - 2)
                    exps(j, j % 3)
                seen(max_ready, n), seen(turned, n)

            def turn_heads(self):
                act, seen = self.act, self.seen
                for t in range(ST):
                    for b in range(2):
                        act.wait_ge(heads_turned, seen(heads_turned))
                        self.f(r(zh[:, 4 * b:4 * b + 4, t * P:t * P + P]), ps[:, 2 * t + b, :].rearrange("p (k q) -> p k q", k=4),
                               ACT.Copy).then_inc(heads_ready, 1)

            def residual(self, T, g):
                self.res_per = 2 * T // S

            def conv(self):
                act, seen = self.act, self.seen
                for n in range(KT):
                    self.ahead(4)
                    self.take_rows()
                    self.used(4)
                    if n >= 2:
                        act.wait_ge(conv_taken, seen.now(conv_taken) + n - 1)
                    self.f(gated[:, n % 2, :], ps[:, 2 * (n % 2) + 1, :], ACT.Sigmoid,
                           bias=c("pw1_b")[:, KT + n:KT + n + 1]).then_inc(sig_ready, 1)
                    self.fill(6, 7)
                seen(conv_taken, KT)
                self.fill(6, 7)
                for k in range(0, KT, 2):
                    act.wait_ge(dev_ready, seen(dev_ready))
                    self.f(square[:, k:k + 2, :], conv_out[:, k:k + 2, :], ACT.Square).then_inc(sq_ready, 1)
                self.take_rows()
                act.wait_ge(stat_ready, seen(stat_ready, 2))
                self.f(std[:], ps[:, 1, :], ACT.Sqrt, bias=c("eps")[:, 2:3]).then_inc(std_ready, 1)
                self.fill(6, 7)
                for k in range(KT):
                    act.wait_ge(scaled_ready, seen(scaled_ready))
                    self.f(conv_out[:, k, :], conv_out[:, k, :], ACT.Silu, bias=c("conv_ln_b")[:, k:k + 1]).then_inc(act_step, 1)
                    act.wait_ge(act_step, seen(act_step))
                    self.f(r(zh[:, k, :]), conv_out[:, k, :], ACT.Copy).then_inc(norm_ready, 1)
                self.take_rows()
                self.last_product()

            def attention(self):
                act, seen = self.act, self.seen
                for n in range(5):
                    self.used(4)
                    if n < 4:
                        self.f(q_at[:, 2 * n:2 * n + 2, :], ps[:, n, :], ACT.Copy, scale=64 ** -0.5).then_inc(proj_ready, 1)
                    else:
                        for d in range(2):
                            self.f(k_at[:, d, :], ps[:, 4 + d, :], ACT.Copy).then_inc(proj_ready, 1)
                self.used(4)
                for i in range(2):
                    ins = self.f(v_at[:, 2 * i:2 * i + 2, :], ps[:, 6 + i, :], ACT.Copy)
                ins.then_inc(val_ready, 1)
                self.ahead()

                def exps(j, b):
                    self.f(probs[:, b, :], ps[:, b, :], ACT.Exp, bias=neg_max[:, j, 0:1], accum_out=sums[:, j, 0:1]).then_inc(exp_done, 1)
                    t, p, g, i = JOBS2[j]
                    h = 4 * (2 * p + i) + g
                    self.f(sink_e[:, j:j + 1], c("sink")[:, h:h + 1], ACT.Exp, bias=neg_max[:, j, 0:1]).then_inc(sink_ready, 1)

                self.jobs(len(JOBS2), exps)
                self.turn_heads()
                self.last_product()

            def finish(self):
                act, seen = self.act, self.seen
                for k in range(0, KT, 2):
                    act.wait_ge(res_ready, seen(res_ready, self.res_per))
                    self.f(square[:, k:k + 2, 0:S], x[:, k:k + 2, 0:S], ACT.Square).then_inc(sq_ready, 1)
                act.wait_ge(stat_ready, seen(stat_ready))
                self.f(std[:, 0:S], ps[:, 0, 0:S], ACT.Sqrt, bias=c("eps")[:, 2:3]).then_inc(std_ready, 1)

        @block.scalar
        def _(act):
            stages(Act(act))

        class Dve:
            def __init__(self, dve):
                self.dve, self.seen, self.steps = dve, Seen(), 0
                self.q = 0
                self.s = 0
                self.n = 0
                self.fills = 0
                self.taken = 0

            def start(self):
                v = self.dve
                nc.vector.memset(gated[:, :, :], 0.0).then_inc(hidden_ready, RING)
                nc.vector.memset(row_buf[:, :], 0.0).then_inc(quarter_done, RING)
                for buf in (block_kv, hid4, vc_diag, sc):
                    self.link(nc.vector.memset(buf[:], 0.0))
                v.wait_ge(x_landed, 16)

            def link(self, ins):
                self.steps += 1
                ins.then_inc(dve_step, 1)
                self.dve.wait_ge(dve_step, self.steps)

            def low(self, lap=None):
                q = self.s
                self.s += 1
                if q >= len(RAW) or RAW[q]:
                    return
                self.n += 1
                self.dve.wait_ge(high_ready, self.n if lap is None else lap * (4 * STEPS) + self.n)
                self.tt(r(low[:, q % RING, :]), raw[:, q % RING, :], high[:, q % RING, :], ALU.subtract).then_inc(low_ready, 1)

            def ahead(self, n=0):
                while self.s < self.q + n + AHEAD:
                    self.low()

            def used(self, n):
                self.ahead(n)
                self.q += n
                self.dve.wait_ge(quarter_done, self.q + RING)

            def tt(self, out, a, b, op):
                return nc.vector.tensor_tensor(out, a, b, op)

            def stt(self, out, a, s, b, op0, op1):
                return nc.vector.scalar_tensor_tensor(out, a, s, b, op0, op1)

            def ts(self, out, a, s1, s2, op0, op1=None):
                return nc.vector.tensor_scalar(out, a, s1, s2, op0, op1) if op1 is not None else nc.vector.tensor_scalar(out, a, s1, None, op0)

            def split_x(self, T):
                self.lows(T, x)
                self.ahead()
                self.dve.wait_ge(consts_landed, 16)

            def lows(self, T, src):
                for k, h, cols in pieces(T):
                    self.dve.wait_ge(norm_ready, self.seen(norm_ready))
                    self.tt(r(zl[:, k, cols]), src[:, k, cols], zh[:, k, cols], ALU.subtract).then_inc(in_ready, 1)

            def ffn(self, T):
                v, seen = self.dve, self.seen
                self.ahead()
                w0, n0, q0 = self.s, self.n, self.q
                s0 = seen.now(silu_ready)
                h = hidden[:].rearrange("p (i j) n -> p i j n", i=LOOPS)
                with v.Fori(0, LOOPS) as i:
                    for j in range(STEPS):
                        for _ in range(4):
                            self.low(i)
                        v.wait_ge(silu_ready, i * STEPS + (s0 + j + 1))
                        up = ps[:, 2 * (j % 2) + 1, :] if T == 512 else ps[:, j % 4, S:512]
                        self.tt(h[:, i, j, 0:T], gated[:, j % 2, 0:T], up, ALU.mult).then_inc(hidden_ready, 1)
                self.s, self.n, self.q = w0 + 4 * FT, n0 + 4 * FT, q0 + 4 * FT
                seen(silu_ready, FT)
                for f in range(FT):
                    v.wait_ge(h_high, seen(h_high))
                    self.tt(r(h_split[:, f % 2, 1, 0:T]), hidden[:, f, 0:T], h_split[:, f % 2, 0, 0:T], ALU.subtract).then_inc(h_low, 1)
                    while self.s < self.q + 2 * (f - 1) + AHEAD:
                        self.low()
                self.q += 2 * FT
                self.ahead()
                v.wait_ge(quarter_done, self.q + RING)

            def take_cols(self, bank):
                if self.taken == self.fills:
                    return
                g = self.taken % GROUPS
                self.taken += 1
                self.dve.wait_ge(rows_turned, self.taken)
                nc.vector.tensor_copy(mods_raw[:].rearrange("p a k c -> p (a k c)")[:, 8 * g:8 * g + 8], ps[:, bank, 0:8]).then_inc(cols_taken, 1)

            def fill(self, rows=4, cols=6):
                self.take_cols(cols)
                self.q += KT
                self.fills += 1

            def post_norm(self, scale, eps, g, b):
                v, seen = self.dve, self.seen
                for n in range(4):
                    self.stt(wide[:, 2 * n:2 * n + 2, 0:S], x[:, 2 * n:2 * n + 2, 0:S], scale, y_bank(n), ALU.mult, ALU.add).then_inc(z_ready, 1)
                v.wait_ge(z_ready, seen(z_ready, 4))
                v.wait_ge(stat_ready, seen(stat_ready))
                for n in range(4):
                    self.tt(wide[:, 2 * n:2 * n + 2, 0:S], wide[:, 2 * n:2 * n + 2, 0:S],
                            ps[:, 0, 0:S].unsqueeze(1).broadcast_to([P, 2, S]), ALU.subtract).then_inc(dev_ready, 1)
                self.fill()
                v.wait_ge(dev_ready, seen(dev_ready, 4))
                seen(stat_ready)
                self.ahead()
                v.wait_ge(std_ready, seen(std_ready))
                self.link(nc.vector.reciprocal(rstd[:, 0:S], std[:, 0:S]))
                for m in range(KT + 2):
                    if m < KT:
                        self.stt(x[:, m, 0:S], wide[:, m, 0:S], g[:, m:m + 1], rstd[:, 0:S], ALU.mult, ALU.mult).then_inc(scaled_ready, 1)
                    if m >= 2:
                        k = m - 2
                        v.wait_ge(norm_ready, seen(norm_ready))
                        self.tt(r(zl[:, k, 0:S]), x[:, k, 0:S], zh[:, k, 0:S], ALU.subtract).then_inc(in_ready, 1)
                self.fill()
                self.ahead()

            def pre_norm(self, T, n, l):
                v, seen = self.dve, self.seen
                if l == 0:
                    self.fill(1, 2)
                self.ahead()
                v.wait_ge(std_ready, seen(std_ready))
                seen(stat_ready)
                self.link(nc.vector.reciprocal(rstd[:, 0:T], std[:, 0:T]))
                items = pieces(T)
                for m in range(len(items) + 2):
                    if m < len(items):
                        k, h, cols = items[m]
                        self.stt(wide[:, k, cols], x[:, k, cols], mod_a[:, n, k, h:h + 1], rstd[:, cols], ALU.mult, ALU.mult).then_inc(scaled_ready, 1)
                    if m >= 2:
                        k, h, cols = items[m - 2]
                        v.wait_ge(norm_ready, seen(norm_ready))
                        self.tt(r(zl[:, k, cols]), wide[:, k, cols], zh[:, k, cols], ALU.subtract).then_inc(in_ready, 1)
                if l == 0:
                    self.fill()
                self.ahead()

            def modulation(self, l):
                v, seen = self.dve, self.seen
                v.wait_ge(rest_landed, 32)
                if l == 0:
                    self.take_cols(6)
                    v.wait_ge(cols_taken, self.taken)
                    self.fill()
                else:
                    self.fill()
                    self.take_cols(6)
                    v.wait_ge(cols_taken, self.taken)
                b = c(f"ada_b{l}").unsqueeze(2).broadcast_to([P, NMOD * KT, 2])
                self.link(self.tt(mods[:].rearrange("p a k c -> p (a k) c"), mods_raw[:].rearrange("p a k c -> p (a k) c"), b, ALU.add))
                for n in range(3):
                    gn = c(f"norm_g{l}")[:, n * KT:n * KT + KT].unsqueeze(2).broadcast_to([P, KT, 2])
                    self.stt(mod_a[:, n], mods[:, 3 * n + 1], 1.0, gn, ALU.add, ALU.mult)
                for n in (2, 8):
                    i = self.ts(mods[:, n], mods[:, n], 0.5, None, ALU.mult)
                i.then_inc(mods_ready, 1)
                v.wait_ge(mods_ready, seen(mods_ready))

            def ple(self, l):
                v, seen = self.dve, self.seen
                for d in range(4):
                    self.ahead(4)
                    self.q += 4
                    v.wait_ge(quarter_done, self.q + RING)
                self.used(4)
                for n in range(4):
                    v.wait_ge(sig_ready, seen(sig_ready, 2))
                    self.link(self.tt(square[:, 2 * n:2 * n + 2, 0:S], square[:, 2 * n:2 * n + 2, 0:S], y_bank(n), ALU.mult))
                    self.tt(x[:, 2 * n:2 * n + 2, 0:S], x[:, 2 * n:2 * n + 2, 0:S], square[:, 2 * n:2 * n + 2, 0:S], ALU.add).then_inc(res_ready, 1)
                v.wait_ge(res_ready, seen(res_ready, 4))
                self.fill()

            def rotate(self, x2, bank, name):
                cos, sin = (c(f"{name}_{n}").unsqueeze(1).broadcast_to([P, 2, S]) for n in ("cos", "sin"))
                v, seen = self.dve, self.seen
                v.wait_ge(swapped, seen(swapped))
                t = tmp[:, 0, :].rearrange("p (a s) -> p a s", a=2)
                self.tt(t, ps[:, bank, :].rearrange("p (a s) -> p a s", a=2), sin, ALU.mult)
                self.link(self.tt(x2, x2, cos, ALU.mult))
                self.tt(x2, x2, t, ALU.add).then_inc(rope_ready, 1)
                v.wait_ge(rope_ready, seen(rope_ready))

            def mixer(self, l):
                v, seen = self.dve, self.seen
                lam_init = 0.8 - 0.6 * math.exp(-0.3 * l)
                self.ahead(8)
                lp = c(f"lam{l}").rearrange("p (a b) -> p a b", a=4)
                self.link(self.tt(lam_t[:].rearrange("p (a b) -> p a b", a=2), lp[:, 0:4:2, :], lp[:, 1:4:2, :], ALU.mult))
                nc.vector.tensor_reduce(lam_s[:, 0:2], lam_t[:].rearrange("p (a b) -> p a b", a=2), AX.X, ALU.add).then_inc(lam_in, 1)
                self.ts(subg[:], c(f"subln{l}"), 1.0 - lam_init, None, ALU.mult)
                v.wait_ge(proj_ready, seen(proj_ready, 2))
                self.q += 8
                self.link(self.ts(fl[:, 3, :], proj[0:8, T_FORGET, :], c(f"fox_b{l}", slice(0, 8)), None, ALU.add))
                self.ts(fl[:, 2, :], fl[:, 3, :], 0.0, None, ALU.min).then_inc(forget_in, 1)
                raw = proj[:, T_CMP, :]
                for half in range(2):
                    rows = slice(64 * half, 64 * half + 64)
                    a = raw[rows, :]
                    window = bass.AP(a.tensor, a.offset, [list(a.ap[0]), [1, CMP_BLOCK], [CMP_STRIDE, NC]])
                    pos = c(f"pos{l}", rows).unsqueeze(2).broadcast_to([64, CMP_BLOCK, NC])
                    self.tt(block_kv[rows, :, NC * half:NC * half + NC], window, pos, ALU.add).then_inc(blocks_ready, 1)
                for n in range(7):
                    self.used(4)
                for n in range(3):
                    self.used(4)
                    nc.vector.tensor_copy(val[:, :, 256 * n:256 * n + 256], ps[:, (9 + n) % 4, :].rearrange("p (r m) -> p r m", r=2)).then_inc(val_ready, 1)
                v.wait_ge(proj_ready, seen(proj_ready, 7))
                self.rotate(proj[:, T_KSLC:T_KSLC + 2, :], 4, "nsa")
                self.rotate(proj[:, T_NQ:T_NQ + 2, :], 5, "nsa")
                self.rotate(proj[:, T_DQ:T_DQ + 2, :], 6, "diff")
                self.rotate(proj[:, T_DK:T_DK + 2, :], 7, "diff")
                v.wait_ge(forget_act, seen(forget_act))
                self.link(self.tt(fl[:, 3, :], fl[:, 1, :], fl[:, 2, :], ALU.subtract))
                nc.vector.tensor_tensor_scan(forget, fl[:, 3, :], fl[:, 3, :], 0.0, ALU.add, ALU.bypass).then_inc(forget_ready, 1)
                v.wait_ge(lam_act, seen(lam_act))
                self.link(self.stt(lam_s[:, 2:3], lam_s[:, 1:2], -lam_init, lam_s[:, 0:1], ALU.add, ALU.subtract))
                self.used(16)
                self.ahead(2)
                v.wait_ge(hid_ready, seen(hid_ready))
                nc.vector.tensor_copy(hid4[:, :, :, 0:NC], hid[:, :, NC:2 * NC].unsqueeze(2).broadcast_to([P, 2, 4, NC])).then_inc(hid4_ready, 1)
                self.used(2)
                nc.vector.tensor_copy(val[:, :, 768:896], ps[:, 1:3, 0:P]).then_inc(val_ready, 1)
                self.used(2)
                for h in range(4):
                    i = nc.vector.tensor_copy(vc_diag[32 * h:32 * h + 32, 64 * h:64 * h + 64], ps[32 * h:32 * h + 32, 5, 0:64])
                i.then_inc(kc_ready, 1)
                v.wait_ge(kc_swapped, seen(kc_swapped))
                self.link(self.tt(kc_t[:], ps[:, 4, 0:NC], c("kc_sin"), ALU.mult))
                self.link(self.tt(kc[:], kc[:], c("kc_cos"), ALU.mult))
                self.tt(kc[:], kc[:], kc_t[:], ALU.add).then_inc(kc_ready, 1)
                v.wait_ge(cmp_scores, seen(cmp_scores))
                add = c("cmp_add").rearrange("p (t c) -> p t c", t=ST).unsqueeze(2).broadcast_to([P, ST, 2, NC])
                for i in range(2):
                    src = ps[:, 5 + i, 0:64].rearrange("p (t s c) -> p t s c", t=ST, s=2)[:, :, :, 0:NC]
                    self.link(self.tt(sc[:, :, i:4:2, 0:NC], src, add, ALU.add))
                s3 = sc[:].rearrange("p t h c -> p (t h) c")[:, :, 0:NC]
                self.link(nc.vector.tensor_reduce(cmp_m[:], s3, AX.X, ALU.max))
                self.tt(s3, s3, cmp_m[:].unsqueeze(2).broadcast_to([P, 8, NC]), ALU.subtract).then_inc(cmp_in, 1)
                v.wait_ge(cmp_exp, seen(cmp_exp))
                self.link(nc.vector.tensor_reduce(cmp_s[:], s3, AX.X, ALU.add))
                self.link(nc.vector.reciprocal(cmp_m[:], cmp_s[:]))
                for t in range(ST):
                    mul = c("cmp_mul")[:, t * NC:t * NC + NC].unsqueeze(1).broadcast_to([P, 4, NC])
                    i = self.tt(sc[:, t, :, 0:NC], sc[:, t, :, 0:NC], mul, ALU.mult)
                i.then_inc(cmp_probs, 1)
                self.fill(0, 1)
                g = gates[:].rearrange("p t (h b) -> p t h b", h=4)
                self.link(self.tt(cmp_s[:].rearrange("p (t h) -> p t h", t=ST), cmp_m[:].rearrange("p (t h) -> p t h", t=ST), g[:, :, :, 0], ALU.mult))
                self.fill(4, 3)
                self.ahead()
                v.wait_ge(cmp_out, seen(cmp_out))
                for t in range(ST):
                    i = self.tt(heads[:, t, 0:256].rearrange("p (h d) -> p h d", h=4), ps[:, 7, t * 256:t * 256 + 256].rearrange("p (h d) -> p h d", h=4),
                                cmp_s[:, 4 * t:4 * t + 4].unsqueeze(2).broadcast_to([P, 4, 64]), ALU.mult)
                self.link(i)

                def maxima(j, b):
                    t = JOBS[j][0]
                    nc.vector.tensor_reduce(neg_max[:, j, :], ps[:, b, :].rearrange("p (m k) -> p m k", m=2)[:, :, 0:(t + 1) * P],
                                            AX.X, ALU.max, negate=True).then_inc(max_ready, 1)

                def take(j, b):
                    t, maps, kind, at = JOBS[j]
                    self.link(nc.vector.reciprocal(coef[:, j, :], sums[:, j, :]))
                    if kind in ("slc", "win"):
                        h = at // 64
                        self.link(self.tt(coef[:, j, :], coef[:, j, :], g[:, t, h:4:2, 1 if kind == "slc" else 2], ALU.mult))
                    if kind == "diff1":
                        self.link(self.ts(coef[:, j, :], coef[:, j, :], lam_s[:, 2:3], None, ALU.mult))
                    one = heads[:, t, at:at + 64]
                    dst = bass.AP(one.tensor, one.offset, [list(one.ap[0]), [P, 2], [1, 64]])
                    src = ps[:, 5 + b, 0:P].rearrange("p (m d) -> p m d", m=2)
                    cf = coef[:, j, :].unsqueeze(2).broadcast_to([P, 2, 64])
                    v.wait_ge(out_ready, seen(out_ready))
                    if kind in ("fox", "diff0"):
                        self.tt(dst, src, cf, ALU.mult).then_inc(out_taken, 1)
                    else:
                        half = tmp[:, 0, 0:P].rearrange("p (m d) -> p m d", m=2)
                        self.tt(half, src, cf, ALU.mult).then_inc(out_taken, 1)
                        v.wait_ge(out_taken, self.taken0 + j + 1)
                        self.link(self.tt(dst, dst, half, ALU.add))

                def copy(j, b):
                    n = 2 * (JOBS[j][0] + 1) * P
                    nc.vector.tensor_copy(probs_t[:, b, 0:n], ps[:, 3 + b, 0:n]).then_inc(probs_t_ready, 1)

                self.jobs(len(JOBS), maxima, copy, take)
                sq = tmp[:].rearrange("p a (h d) -> p a h d", h=8)[:, :, 0:4, :]
                od = heads[:, :, 256:512].rearrange("p t (h d) -> p t h d", h=4)
                for t in range(ST):
                    i = self.tt(sq[:, t], od[:, t], od[:, t], ALU.mult)
                self.link(i)
                nc.vector.tensor_reduce(rms[:].rearrange("p (t h) -> p t h", t=ST), sq, AX.X, ALU.add).then_inc(rms_in, 1)
                v.wait_ge(rms_act, seen(rms_act))
                self.link(nc.vector.reciprocal(rms[:], rms[:]))
                for t in range(ST):
                    self.link(self.tt(od[:, t], od[:, t], rms[:, 4 * t:4 * t + 4].unsqueeze(2).broadcast_to([P, 4, 64]), ALU.mult))
                    i = self.tt(od[:, t], od[:, t], subg[:].unsqueeze(1).broadcast_to([P, 4, 64]), ALU.mult)
                i.then_inc(heads_whole, 1)
                self.turn_heads()
                self.last_product()

            def turn_heads(self):
                v, seen = self.dve, self.seen
                for t in range(ST):
                    for b in range(2):
                        v.wait_ge(heads_ready, seen(heads_ready))
                        rows = slice(t * P, t * P + P)
                        self.tt(r(zl[:, 4 * b:4 * b + 4, rows]), ps[:, 2 * t + b, :].rearrange("p (k q) -> p k q", k=4),
                                zh[:, 4 * b:4 * b + 4, rows], ALU.subtract).then_inc(in_ready, 1)

            def last_product(self):
                for n in range(4):
                    self.used(4)

            def jobs(self, n, maxima, copy, take):
                v, seen = self.dve, self.seen
                s0, t0 = seen.now(score_ready), seen.now(turned)
                self.taken0 = seen.now(out_taken)
                for j in range(n + 2):
                    if j < n:
                        v.wait_ge(score_ready, s0 + j + 1)
                        maxima(j, j % 3)
                    if 1 <= j <= n:
                        v.wait_ge(turned, t0 + j)
                        copy(j - 1, (j - 1) % 2)
                    if j >= 2:
                        take(j - 2, (j - 2) % 2)
                v.wait_ge(out_taken, seen(out_taken, n))
                seen(score_ready, n), seen(turned, n)

            def residual(self, T, g):
                v, seen = self.dve, self.seen
                for k, h, cols in pieces(T):
                    self.stt(x[:, k, cols], y_tile(T, k)[:, cols], mods[:, g, k, h:h + 1], x[:, k, cols], ALU.mult, ALU.add).then_inc(res_ready, 1)
                v.wait_ge(res_ready, seen(res_ready, KT * T // S))

            def conv(self):
                v, seen = self.dve, self.seen
                for n in range(KT):
                    nc.vector.memset(conv_in[:, n, :, 0:PAD], 0.0)
                    i = nc.vector.memset(conv_in[:, n, :, PAD + S:], 0.0)
                self.link(i)
                w = c("conv_w").rearrange("p (k t) -> p k t", k=KT)
                for n in range(KT):
                    self.used(4)
                    v.wait_ge(sig_ready, seen(sig_ready))
                    self.stt(conv_in[:, n, :, PAD:PAD + S], ps[:, 2 * (n % 2), :].rearrange("p (a s) -> p a s", a=2), c("pw1_b")[:, n:n + 1],
                             gated[:, n % 2, :].rearrange("p (a s) -> p a s", a=2), ALU.add, ALU.mult).then_inc(conv_taken, 1)
                    v.wait_ge(conv_taken, seen(conv_taken))
                    self.fill(6, 7)
                    acc = ps[:, 4 + n % 2, :].rearrange("p (a s) -> p a s", a=2)
                    self.link(self.ts(acc, conv_in[:, n, :, 0:S], w[:, n, 0:1], c("conv_b")[:, n:n + 1], ALU.mult, ALU.add))
                    for t in range(1, TAPS):
                        last = t == TAPS - 1
                        dst = conv_out[:, n, :].rearrange("p (a s) -> p a s", a=2) if last else acc
                        i = self.stt(dst, conv_in[:, n, :, t:t + S], w[:, n, t:t + 1], acc, ALU.mult, ALU.add)
                        if last:
                            i.then_inc(z_ready, 1)
                        else:
                            self.link(i)
                        if t in (4, 10, 16, 22) and n < KT - 1:
                            self.low_of_next_tile()
                v.wait_ge(z_ready, seen(z_ready, KT))
                v.wait_ge(stat_ready, seen(stat_ready))
                for k in range(0, KT, 2):
                    self.tt(conv_out[:, k:k + 2, :], conv_out[:, k:k + 2, :], ps[:, 0, :].unsqueeze(1).broadcast_to([P, 2, 512]), ALU.subtract).then_inc(dev_ready, 1)
                self.fill(6, 7)
                v.wait_ge(dev_ready, seen(dev_ready, 4))
                seen(stat_ready)
                v.wait_ge(std_ready, seen(std_ready))
                self.link(nc.vector.reciprocal(rstd[:], std[:]))
                for k in range(KT):
                    self.stt(conv_out[:, k, :], conv_out[:, k, :], c("conv_ln_g")[:, k:k + 1], rstd[:], ALU.mult, ALU.mult).then_inc(scaled_ready, 1)
                self.fill(6, 7)
                for k in range(KT):
                    v.wait_ge(norm_ready, seen(norm_ready))
                    self.tt(r(zl[:, k, :]), conv_out[:, k, :], zh[:, k, :], ALU.subtract).then_inc(in_ready, 1)
                self.ahead()
                self.link(self.tt(cmp_s[:], c("pw2_b"), mods[:, 5, :, 0], ALU.mult))
                self.link(self.tt(cmp_m[:], c("pw2_b"), mods[:, 5, :, 1], ALU.mult))
                for k, h, cols in pieces(512):
                    i = self.ts(x[:, k, cols], x[:, k, cols], (cmp_s, cmp_m)[h][:, k:k + 1], None, ALU.add)
                self.link(i)
                self.last_product()

            def low_of_next_tile(self):
                if self.s < self.q + KT + 4 + AHEAD:
                    self.low()

            def attention(self):
                v, seen = self.dve, self.seen
                for n in range(6):
                    self.used(4)
                v.wait_ge(proj_ready, seen(proj_ready, 6))
                self.ahead()
                for n in range(4):
                    self.rotate(q_at[:, 2 * n:2 * n + 2, :], n, "ax")
                self.rotate(k_at[:, :, 0:S], 4, "ax")

                def maxima(j, b):
                    t, p, g, i = JOBS2[j]
                    h = 4 * (2 * p + i) + g
                    self.link(nc.vector.tensor_reduce(coef[:, j, 0:1], ps[:, b, :], AX.X, ALU.max))
                    self.ts(neg_max[:, j, 0:1], coef[:, j, 0:1], c("sink")[:, h:h + 1], -1.0, ALU.max, ALU.mult).then_inc(max_ready, 1)

                def copy(j, b):
                    nc.vector.tensor_copy(probs_t[:, b, :], ps[:, 3 + b, :]).then_inc(probs_t_ready, 1)

                def take(j, b):
                    t, p, g, i = JOBS2[j]
                    h = 4 * (2 * p + i) + g
                    v.wait_ge(sink_ready, seen(sink_ready))
                    self.link(self.tt(sums[:, j, 0:1], sums[:, j, 0:1], sink_e[:, j:j + 1], ALU.add))
                    self.link(nc.vector.reciprocal(coef[:, j, 1:2], sums[:, j, 0:1]))
                    v.wait_ge(out_ready, seen(out_ready))
                    self.ts(heads[:, t, 64 * h:64 * h + 64], ps[:, 5 + b, 0:64], coef[:, j, 1:2], None, ALU.mult).then_inc(out_taken, 1)

                self.jobs(len(JOBS2), maxima, copy, take)
                self.ts(rms[:, 0:1], coef[:, 0, 0:1], 1.0, None, ALU.mult).then_inc(heads_whole, 1)
                self.turn_heads()
                self.last_product()

            def finish(self):
                v, seen = self.dve, self.seen
                v.wait_ge(std_ready, seen(std_ready))
                self.link(nc.vector.reciprocal(rstd[:, 0:S], std[:, 0:S]))
                for k in range(KT):
                    i = self.stt(wide[:, k, 0:S], x[:, k, 0:S], c("final_g")[:, k:k + 1], rstd[:, 0:S], ALU.mult, ALU.mult)
                i.then_inc(result_ready, 1)

        @block.vector
        def _(dve):
            stages(Dve(dve))

        @block.gpsimd
        def _(pool):
            pool.dma_start(ple_p[:], p_in).then_inc(rest_landed, 16)
            pool.dma_start(x[:, :, S:512], ctx_in).then_inc(rest_landed, 16)
            pool.wait_ge(result_ready, 1)
            pool.wait_ge(rest_landed, 32)
            pool.dma_start(out, wide[:, :, 0:S]).then_inc(stored, 16)
            pool.wait_ge(stored, 16)


def kernel(**inputs):
    import concourse.bacc as bacc
    from concourse.bass_utils import run_bass_kernel_spmd

    inp = {k: np.asarray(v) for k, v in inputs.items()}
    weights = lay_weights(inp)
    n_quarters = weights.shape[0]
    arrays = {
        "weights": weights,
        "consts": lay_constants(inp),
        "x_in": lay_rows(inp["x"]),
        "ctx_in": lay_rows(inp["ctx_2"]),
        "p_in": np.ascontiguousarray(np.stack([inp["p"][l, 0].T.reshape(2, P, S).transpose(1, 0, 2) for l in range(DEPTH)], 1)),
    }
    nc = bacc.Bacc("TRN2", target_bir_lowering=False, num_devices=1)
    aps = {n: nc.dram_tensor(n, a.shape, F32, kind="ExternalInput").ap() for n, a in arrays.items()}
    out = nc.dram_tensor("out", (P, KT, S), F32, kind="ExternalOutput").ap()
    build(nc, aps["weights"], aps["consts"], aps["x_in"], aps["ctx_in"], aps["p_in"], out, n_quarters)
    res = run_bass_kernel_spmd(nc, [arrays], core_ids=[0])
    got = res.results[0]["out"]
    return np.ascontiguousarray(got.transpose(1, 0, 2).reshape(D, S).T)[None]
```
